# Optimizing a Trainium2 kernel written in Bass

```python
import jax, jax.numpy as jnp
from jax import lax
import numpy as np

D_MODEL = 1024
BATCH = 1
SEQ = 512
DEPTH = 1

HEAD_DIM = 64
SB_HEADS = 8
DIL_GROUPS = ((128, 1), (512, 4), (2048, 16))
DIL_KV_HEADS = 4
DIL_Q_HEADS = DIL_KV_HEADS * len(DIL_GROUPS)
D_FF = 2816
ROPE_THETA = 10000.0
RMS_EPS = 1e-6
Q_BLOCK = 128

SB_W = SB_HEADS * HEAD_DIM
DQ_W = DIL_Q_HEADS * HEAD_DIM
DKV_W = DIL_KV_HEADS * HEAD_DIM
IN_SIZES = (SB_W, SB_W, SB_W, DQ_W, DKV_W, DKV_W, 2 * D_MODEL)
IN_WIDTH = SB_W * 3 + DQ_W + 2 * DKV_W + 2 * D_MODEL

kernel_name = "hybrid_stickbreak_dilated_macaron"

def rmsnorm(x, g):
    xf = x.astype(jnp.float32)
    y = xf * lax.rsqrt(jnp.mean(xf * xf, axis=-1, keepdims=True) + RMS_EPS)
    return (y * g.astype(jnp.float32)).astype(x.dtype)

def swiglu(h, w1, w3, w2):
    return (jax.nn.silu(h @ w1) * (h @ w3)) @ w2

def split_heads(t, n):
    b, s, _ = t.shape
    return t.reshape(b, s, n, HEAD_DIM).transpose(0, 2, 1, 3)

def merge_heads(t):
    b, h, s, dh = t.shape
    return t.transpose(0, 2, 1, 3).reshape(b, s, h * dh)

def rope(t):
    s, dh = t.shape[2], t.shape[3]
    half = dh // 2
    inv_freq = ROPE_THETA ** (-jnp.arange(half, dtype=jnp.float32) / half)
    ang = jnp.arange(s, dtype=jnp.float32)[:, None] * inv_freq[None, :]
    cos, sin = jnp.cos(ang), jnp.sin(ang)
    tf = t.astype(jnp.float32)
    t1, t2 = tf[..., :half], tf[..., half:]
    out = jnp.concatenate([t1 * cos - t2 * sin, t2 * cos + t1 * sin], axis=-1)
    return out.astype(t.dtype)

def stick_breaking_attention(q, k, v):
    s_len = q.shape[2]
    scale = HEAD_DIM ** -0.5
    outs = []
    for i in range(s_len // Q_BLOCK):
        t0, end = i * Q_BLOCK, (i + 1) * Q_BLOCK
        qb, kb, vb = q[:, :, t0:end], k[:, :, :end], v[:, :, :end]
        z = jnp.einsum('bhqd,bhkd->bhqk', qb, kb).astype(jnp.float32) * scale
        t_pos = t0 + jnp.arange(Q_BLOCK)[:, None]
        s_pos = jnp.arange(end)[None, :]
        strict = s_pos < t_pos
        log_not = jnp.where(strict, jax.nn.log_sigmoid(-z), 0.0)
        between = lax.cumsum(log_not, axis=3, reverse=True) - log_not
        a = jnp.where(strict, jnp.exp(jax.nn.log_sigmoid(z) + between), 0.0)
        outs.append(jnp.einsum('bhqk,bhkd->bhqd', a.astype(vb.dtype), vb))
    return jnp.concatenate(outs, axis=2)

def dilated_window_attention(q, k, v):
    b, _, s_len, dh = q.shape
    n_groups = len(DIL_GROUPS)
    nb = s_len // Q_BLOCK
    scale = HEAD_DIM ** -0.5
    qg = q.reshape(b, n_groups, DIL_KV_HEADS, nb, Q_BLOCK, dh).transpose(3, 1, 0, 2, 4, 5)

    def block(args):
        qblk, t0 = args
        t_pos = t0 + jnp.arange(Q_BLOCK)
        outs, lses = [], []
        for g, (window, dil) in enumerate(DIL_GROUPS):
            m = jnp.arange(window // dil + 1)
            idx = t_pos[:, None] - dil * m[None, :]
            valid = idx >= 0
            idx = jnp.maximum(idx, 0)
            kg = jnp.take(k, idx, axis=2)
            vg = jnp.take(v, idx, axis=2)
            sc = jnp.einsum('bhqd,bhqmd->bhqm', qblk[g], kg).astype(jnp.float32) * scale
            sc = jnp.where(valid, sc, -jnp.inf)
            mx = jnp.max(sc, axis=-1, keepdims=True)
            e = jnp.exp(sc - mx)
            den = jnp.sum(e, axis=-1, keepdims=True)
            p = e / den
            outs.append(jnp.einsum('bhqm,bhqmd->bhqd', p.astype(vg.dtype), vg).astype(jnp.float32))
            lses.append(mx + jnp.log(den))
        alpha = jax.nn.softmax(jnp.stack(lses), axis=0)
        return jnp.sum(alpha * jnp.stack(outs), axis=0).astype(v.dtype)

    t0s = jnp.arange(nb, dtype=jnp.int32) * Q_BLOCK
    o = lax.map(block, (qg, t0s))
    return o.transpose(1, 2, 0, 3, 4).reshape(b, DIL_KV_HEADS, s_len, dh)

def setup_inputs(seed: int = 0) -> dict:
    key = jax.random.key(seed)
    ks = jax.random.split(key, 20)

    def w(k, shape, fan_in):
        return jax.random.normal(k, shape, jnp.float32) * fan_in ** -0.5

    def gain(k, shape):
        return 1.0 + 0.05 * jax.random.normal(k, shape, jnp.float32)

    L = DEPTH
    return {
        "x": jax.random.normal(ks[0], (BATCH, SEQ, D_MODEL), jnp.float32),
        "g_ffn1": gain(ks[1], (L, D_MODEL)),
        "w1_a": w(ks[2], (L, D_MODEL, D_FF), D_MODEL),
        "w3_a": w(ks[3], (L, D_MODEL, D_FF), D_MODEL),
        "w2_a": w(ks[4], (L, D_FF, D_MODEL), D_FF),
        "g_mix": gain(ks[5], (L, D_MODEL)),
        "w_in": w(ks[6], (L, D_MODEL, IN_WIDTH), D_MODEL),
        "b_gate": 0.01 * jax.random.normal(ks[7], (L, 2 * D_MODEL), jnp.float32),
        "w_sb_out": w(ks[8], (L, SB_W, D_MODEL), SB_W),
        "w_dil_out": w(ks[9], (L, DKV_W, D_MODEL), DKV_W),
        "w_o": w(ks[10], (L, D_MODEL, D_MODEL), D_MODEL),
        "g_ffn2": gain(ks[11], (L, D_MODEL)),
        "w1_b": w(ks[12], (L, D_MODEL, D_FF), D_MODEL),
        "w3_b": w(ks[13], (L, D_MODEL, D_FF), D_MODEL),
        "w2_b": w(ks[14], (L, D_FF, D_MODEL), D_FF),
        "g_final": gain(ks[15], (D_MODEL,)),
    }

def reference(x, g_ffn1, w1_a, w3_a, w2_a, g_mix, w_in, b_gate, w_sb_out, w_dil_out, w_o,
              g_ffn2, w1_b, w3_b, w2_b, g_final):
    split_points = [int(p) for p in np.cumsum(IN_SIZES)[:-1]]
    for l in range(DEPTH):
        h = rmsnorm(x, g_ffn1[l])
        x = x + 0.5 * swiglu(h, w1_a[l], w3_a[l], w2_a[l])

        h = rmsnorm(x, g_mix[l])
        proj = h @ w_in[l]
        q_sb, k_sb, v_sb, q_dl, k_dl, v_dl, gate_pre = jnp.split(proj, split_points, axis=-1)
        gates = jax.nn.sigmoid(gate_pre + b_gate[l])
        g_sb, g_dl = gates[..., :D_MODEL], gates[..., D_MODEL:]

        y_sb = stick_breaking_attention(split_heads(q_sb, SB_HEADS), split_heads(k_sb, SB_HEADS),
                                        split_heads(v_sb, SB_HEADS))
        y_sb = merge_heads(y_sb) @ w_sb_out[l]

        y_dl = dilated_window_attention(rope(split_heads(q_dl, DIL_Q_HEADS)),
                                        rope(split_heads(k_dl, DIL_KV_HEADS)),
                                        split_heads(v_dl, DIL_KV_HEADS))
        y_dl = merge_heads(y_dl) @ w_dil_out[l]

        x = x + (g_sb * y_sb + g_dl * y_dl) @ w_o[l]

        h = rmsnorm(x, g_ffn2[l])
        x = x + 0.5 * swiglu(h, w1_b[l], w3_b[l], w2_b[l])
    return rmsnorm(x, g_final)


_drawn_inputs = setup_inputs


def setup_inputs(seed=0):
    import zlib

    import numpy as np

    out = dict(_drawn_inputs(seed))
    spreads = {}
    factors = {'b_gate': 31.981, 'g_ffn2': 3.006}
    for name, (base, spread) in spreads.items():
        noise = np.random.default_rng([zlib.crc32(name.encode()), seed]).standard_normal(out[name].shape)
        drawn = base * np.exp(spread * noise) if base else spread * noise
        out[name] = __import__('jax').numpy.asarray(drawn.astype(out[name].dtype))
    for name, factor in factors.items():
        out[name] = (out[name] * factor).astype(out[name].dtype)
    return out
```

```python
from contextlib import ExitStack

import numpy as np

import concourse.bass as bass
from concourse import mybir

P = 128
SEQ = 512
D = 1024
KD = D // P
FF = 2816
NF = FF // P
CHUNKS = ((0, 8), (8, 8), (16, 6))
HD = 64
SB_PAIRS = 4
DL_PAIRS = 2
NG = 3
DIL = 4
BLK = SEQ // P
EPS = 1e-6
NEG = -1e30
RING = 4

FFN_UNITS = 3 * NF + 2
FFN_A = 0
MIX = 2 * NF + len(CHUNKS) * KD
MIX_UNITS = 3 * SB_PAIRS + (NG + 2) * DL_PAIRS
GATE = MIX + MIX_UNITS
END = GATE + KD
WO = END + 3 * KD
FFN_B = WO + KD
UNITS = FFN_B + 2 * NF + len(CHUNKS) * KD
END_COLS = ((0, 1024), (1024, 512), (1536, 256))
SB_BANKS = (((1, 0), (3, 384)), ((2, 0),), ((0, 0),))
SB_WIDTH = (512, 256, 512)
SB_AT = (0, 512, 768)


def chunk_base(base, c):
    return base + sum(2 * n + KD for _, n in CHUNKS[:c])


def unit_width(u):
    for base in (FFN_A, FFN_B):
        for c, (_, n) in enumerate(CHUNKS):
            at = chunk_base(base, c) + 2 * n
            if at <= u < at + KD:
                return n * P
    if END <= u < WO:
        return END_COLS[(u - END) % 3][1]
    return KD * P


def sb_block(i):
    for b, parts in enumerate(SB_BANKS):
        for blk, col in parts:
            if blk == i:
                return b, col


def mix_schedule():
    sb = lambda hp: [MIX + 3 * hp + n for n in range(3)]
    dl = lambda jp: [MIX + 3 * SB_PAIRS + (NG + 2) * jp + n for n in range(NG + 2)]
    q, k, v = sb(0)
    s = [("Ua", q), ("Ub", q), ("norm", 1), ("Ua", k), ("Ub", k), ("fin", q), ("Ua", v), ("Ub", v), ("fin", k)]
    late = v
    for hp in range(SB_PAIRS):
        a, b = 2 * hp, 2 * hp + 1
        s.append(("scores", a))
        if hp:
            s.append(("y", a - 1))
        s.append(("fin", late))
        if hp < SB_PAIRS - 1:
            q, k, v = sb(hp + 1)
            s += [("Ua", q), ("Ub", q), ("suffix", a), ("Ua", k), ("pv", a), ("scores", b), ("y", a),
                  ("Ub", k), ("fin", q), ("Ua", v), ("suffix", b), ("Ub", v), ("fin", k), ("pv", b)]
            late = v
        else:
            u = dl(0)
            s += [("Ua", u[0]), ("Ub", u[0]), ("suffix", a), ("Ua", u[1]), ("Ub", u[1]), ("fin", u[0]), ("pv", a),
                  ("scores", b), ("y", a), ("Ua", u[2]), ("Ub", u[2]), ("fin", u[1]), ("suffix", b),
                  ("Ua", u[3]), ("Ub", u[3]), ("fin", u[2]), ("pv", b), ("y", b), ("Ua", u[4]), ("Ub", u[4]),
                  ("fin", u[3]), ("fin", u[4])]
    fill = []
    for n, u in enumerate(dl(1)):
        fill += [[("Ua", u)], [("Ub", u)] + ([("fin", u - 1)] if n else [])]
    fill[-1].append(("fin", dl(1)[-1]))
    gates = [[(half, u)] for u in range(GATE, END) for half in ("Ua", "Ub")]
    for j in range(2 * DL_PAIRS):
        for r in range(DIL):
            s.append(("dscores", (j, r)))
            if r == 1 and j:
                s.append(("dy", j - 1))
            src = fill if j < 2 else gates
            for _ in range(2 if j >= 2 or r % 4 == 0 else 1):
                if src:
                    s += src.pop(0)
            s.append(("dturn", (j, r)))
        s.append(("dpv", j))
    s.append(("dy", 2 * DL_PAIRS - 1))
    return s


MIX_STEPS = mix_schedule()
FINS = [w for kind, w in MIX_STEPS if kind == "fin"]


def mix_kind(u):
    n = u - MIX
    if n < 3 * SB_PAIRS:
        return ("q", "k", "v")[n % 3], n // 3, 0
    n -= 3 * SB_PAIRS
    g = n % (NG + 2)
    return ("rq" if g < NG else ("rk", "rv")[g - NG]), n // (NG + 2), min(g, NG - 1)


ROPES = [u for u in FINS if mix_kind(u)[0] in ("rq", "rk")]
TURNED = [u for u in FINS if mix_kind(u)[0] not in ("q", "k")]


def build(nc, A, out):
    F32, F32R, BF16 = mybir.dt.float32, mybir.dt.float32r, mybir.dt.bfloat16
    ALU, ACT, AX = mybir.AluOpType, mybir.ActivationFunctionType, mybir.AxisListType
    ctx = ExitStack()
    with ctx:
        def sb(name, shape, dt=F32, where=ctx):
            return where.enter_context(nc.sbuf_tensor(name, shape, dt))

        def sem(name):
            return ctx.enter_context(nc.semaphore(name))

        x = sb("x", [P, KD, SEQ])
        xg_hi = sb("xg_hi", [P, KD, SEQ], F32R)
        xg_lo = sb("xg_lo", [P, KD, SEQ], F32R)
        w_raw = sb("w_raw", [P, RING, KD * P])
        w_hi = sb("w_hi", [P, RING, KD * P], F32R)
        w_lo = sb("w_lo", [P, RING, KD * P], F32R)
        rstd = sb("rstd", [P, SEQ])
        gains = sb("gains", [P, 4, KD])
        bias = sb("bias", [P, 2, KD])
        hbias = sb("hbias", [P, 2, KD])
        ones = sb("ones", [P, P])
        cos = sb("cos", [P, SEQ])
        sin = sb("sin", [P, SEQ])
        rot = sb("rot", [P, P])
        identf = sb("identf", [P, P])
        tri = sb("tri", [P, P], F32R)
        negones = sb("negones", [P, P], F32R)
        identb = sb("identb", [P, P], BF16)
        mask_sb = sb("mask_sb", [P, P], BF16)
        mask_g0 = sb("mask_g0", [P, DIL, SEQ], BF16)
        mask_g12 = sb("mask_g12", [P, 2 * P], BF16)
        rope1 = sb("rope1", [P, SEQ])
        rope2 = sb("rope2", [P, SEQ])
        roped = sb("roped", [P, SEQ])
        rmax = sb("rmax", [P, 2, 4])
        mean, rden, yraw = rope1, rope1, rope2

        with ExitStack() as ffn:
            ssum = sb("ssum", [P, SEQ], F32, ffn)
            sq = sb("sq", [P, 2, SEQ], F32, ffn)
            hid_hi = sb("hid_hi", [P, 8, SEQ], F32R, ffn)
            hid_lo = sb("hid_lo", [P, 8, SEQ], F32R, ffn)
            gate = sb("gate", [P, 2, SEQ], F32, ffn)
            act_gate = sb("act_gate", [P, 2, SEQ], F32, ffn)
            up = sb("up", [P, 2, SEQ], F32, ffn)
            prod = sb("prod", [P, 2, SEQ], F32, ffn)
            trif = prod[:, 1, 0:P]
        with ExitStack() as mix:
            ys_hi = sb("ys_hi", [P, SB_PAIRS, SEQ], F32R, mix)
            ys_lo = sb("ys_lo", [P, SB_PAIRS, SEQ], F32R, mix)
            yd_hi = sb("yd_hi", [P, DL_PAIRS, SEQ], F32R, mix)
            yd_lo = sb("yd_lo", [P, DL_PAIRS, SEQ], F32R, mix)
            with ExitStack() as att:
                raw = sb("raw", [P, 2, SEQ], F32, att)
                with ExitStack() as s:
                    spA_hi = sb("spA_hi", [P, 1280], F32R, s)
                    spA_lo = sb("spA_lo", [P, 1280], F32R, s)
                    ebuf = sb("ebuf", [P, 1280], F32, s)
                    sv_lo = sb("sv_lo", [P, 2, BLK, P], F32R, s)
                pT_hi = sb("pT_hi", [P, DIL, SEQ], F32R, att)
                pT_lo = sb("pT_lo", [P, DIL, SEQ], F32R, att)
                prob = sb("prob", [P, 1, 6 * P], F32, att)
                dq_hi = [None, None]
                dq_lo, dk_hi, dk_lo, dv_hi, dv_lo = ([None, None] for _ in range(5))

                def dl_buffers(jp, where):
                    dq_hi[jp] = sb(f"dq_hi{jp}", [P, NG, SEQ], F32R, where)
                    dq_lo[jp] = sb(f"dq_lo{jp}", [P, NG, SEQ], F32R, where)
                    dk_hi[jp] = sb(f"dk_hi{jp}", [P, SEQ], F32R, where)
                    dk_lo[jp] = sb(f"dk_lo{jp}", [P, SEQ], F32R, where)
                    dv_hi[jp] = sb(f"dv_hi{jp}", [P, DIL, 3, HD], F32R, where)
                    dv_lo[jp] = sb(f"dv_lo{jp}", [P, DIL, 3, HD], F32R, where)
                with ExitStack() as s:
                    sq_hi = sb("sq_hi", [P, 2, SEQ], F32R, s)
                    sq_lo = sb("sq_lo", [P, 2, SEQ], F32R, s)
                    sk_hi = sb("sk_hi", [P, 2, SEQ], F32R, s)
                    sk_lo = sb("sk_lo", [P, 2, SEQ], F32R, s)
                    sv_hi = sb("sv_hi", [P, 2, BLK, P], F32R, s)
                dl_buffers(1, att)
                with ExitStack() as s:
                    dl_buffers(0, s)
                gsb = sb("gsb", [P, KD, SEQ], F32, att)
            with ExitStack() as end:
                mg_hi = sb("mg_hi", [P, KD, SEQ], F32R, end)
                mg_lo = sb("mg_lo", [P, KD, SEQ], F32R, end)
                gdl = sb("gdl", [P, 2, SEQ], F32, end)
                part = sb("part", [P, 2, SEQ], F32, end)

        acc = [ctx.enter_context(nc.psum_tensor(f"acc{i}", [P, SEQ], F32)) for i in range(RING)]
        bank = [ctx.enter_context(nc.psum_tensor(f"bank{i}", [P, SEQ], F32)) for i in range(4)]

        x_loaded = [sem(f"x_loaded{k}") for k in range(KD)]
        const_loaded = sem("const_loaded")
        w_loaded = [sem(f"w_loaded{i}") for i in range(RING)]
        whi_done = sem("whi_done")
        wlo_done = sem("wlo_done")
        unit_done = sem("unit_done")
        acc_read = [sem(f"acc_read{i}") for i in range(RING)]
        consts_made = sem("consts_made")
        sq_done = sem("sq_done")
        xg_hi_done = sem("xg_hi_done")
        xg_lo_done = sem("xg_lo_done")
        sum_done = sem("sum_done")
        gains_loaded = sem("gains_loaded")
        hbias_made = sem("hbias_made")
        sumsq_done = sem("sumsq_done")
        mean_done = sem("mean_done")
        rms_done = sem("rms_done")
        rstd_done = sem("rstd_done")
        silu_done = sem("silu_done")
        prod_done = sem("prod_done")
        hid_hi_done = sem("hid_hi_done")
        hid_lo_done = sem("hid_lo_done")
        raw_done = sem("raw_done")
        turned = sem("turned")
        rope_step = sem("rope_step")
        op_hi_done = sem("op_hi_done")
        op_lo_done = sem("op_lo_done")
        z_done = sem("z_done")
        soft_step = sem("soft_step")
        sp_step = sem("sp_step")
        sp_split = sem("sp_split")
        suffix_done = sem("suffix_done")
        a_done = sem("a_done")
        a_hi_done = sem("a_hi_done")
        a_split = sem("a_split")
        pv_done = sem("pv_done")
        ys_hi_done = sem("ys_hi_done")
        ys_done = sem("ys_done")
        ds_done = sem("ds_done")
        max_step = sem("max_step")
        p_done = sem("p_done")
        psum_step = sem("psum_step")
        pt_turned = sem("pt_turned")
        pt_hi_done = sem("pt_hi_done")
        pt_split = sem("pt_split")
        dv_ones = sem("dv_ones")
        dpv_done = sem("dpv_done")
        dy_step = sem("dy_step")
        yd_hi_done = sem("yd_hi_done")
        yd_done = sem("yd_done")
        gate_done = sem("gate_done")
        merge_step = sem("merge_step")
        mg_hi_done = sem("mg_hi_done")
        mg_lo_done = sem("mg_lo_done")
        y_ready = sem("y_ready")
        out_stored = sem("out_stored")
        N_CONST = 10

        def reads(u0, i):
            n = len([u for u in range(u0 % RING, u0, RING) if not MIX <= u < GATE])
            return n + i

        block = ctx.enter_context(nc.Block())

        @block.sync
        def _(sp):
            def load(u0, i, src):
                s = u0 % RING
                if u0 >= RING:
                    sp.wait_ge(wlo_done, 4 * i + (u0 - RING + 1))
                sp.dma_start(w_raw[:, s, 0:src.shape[-1]], src).then_inc(w_loaded[s], 16)

            def ffn(base, w13, w2, first):
                for c, (f0, n) in enumerate(CHUNKS):
                    u = chunk_base(base, c)
                    i0 = 0
                    if first and c == 0:
                        i0 = 1
                    if i0 == 1:
                        u += RING
                    with sp.Fori(0, n // 2 - i0) as i:
                        for j in range(4):
                            load(u + j, i, w13[4 * i + (2 * f0 + 4 * i0 + j)])
                    u += 4 * (n // 2 - i0)
                    for m in range(KD):
                        load(u + m, 0, w2[m, :, f0 * P:(f0 + n) * P])

            sp.dma_start(gains[:], A["gains"]).then_inc(gains_loaded, 16)
            for k in range(KD):
                sp.dma_start(x[:, k, :], A["xT"][:, k, :]).then_inc(x_loaded[k], 16)
                if k < RING:
                    load(k, 0, A["w13a"][k])
            for t, name in ((bias, "bias"), (cos, "cos"), (sin, "sin"), (rot, "rot"), (identf, "identf"),
                            (trif, "trif"), (identb, "identb"), (mask_sb, "mask_sb"), (mask_g0, "mask_g0"),
                            (mask_g12, "mask_g12")):
                dst = t if name == "trif" else t[:]
                if name[0:4] == "mask" or name == "identb":
                    dst = dst.bitcast(mybir.dt.uint16)
                sp.dma_start(dst, A[name]).then_inc(const_loaded, 16)
            ffn(FFN_A, A["w13a"], A["w2a"], True)
            with sp.Fori(0, (MIX_UNITS - 2) // 4) as i:
                for j in range(4):
                    load(MIX + j, i, A["wmix"][4 * i + j])
            for u in range(GATE - 2, GATE):
                load(u, 0, A["wmix"][u - MIX])
            with sp.Fori(0, KD // 4) as i:
                for j in range(4):
                    load(GATE + j, i, A["wgate"][4 * i + j])
            with sp.Fori(0, KD // 4) as i:
                for j in range(12):
                    c, n = END_COLS[j % 3]
                    load(END + j, 3 * i, A["wend"][4 * i + j // 3, :, c:c + n])
            with sp.Fori(0, KD // 4) as i:
                for j in range(4):
                    load(WO + j, i, A["wo"][4 * i + j])
            ffn(FFN_B, A["w13b"], A["w2b"], False)
            for m in range(KD):
                sp.wait_ge(y_ready, m + 1)
                sp.dma_start(out[:, m, :], x[:, m, :]).then_inc(out_stored, 16)
            sp.wait_ge(out_stored, 16 * KD)

        @block.scalar
        def _(act):
            def split_hi(u0, i, width):
                s = u0 % RING
                act.wait_ge(w_loaded[s], 16 * i + 16 * (u0 // RING + 1))
                if u0 >= RING:
                    act.wait_ge(unit_done, 4 * i + (u0 - RING + 1))
                act.activation(w_hi[:, s, 0:width], w_raw[:, s, 0:width], ACT.Copy).then_inc(whi_done, 1)

            def square(m, n):
                if m >= 3:
                    act.wait_ge(sum_done, (KD - 1) * n + m - 2)
                dst = sq[:, m % 2, :] if m else ssum[:]
                act.activation(dst, x[:, m, :], ACT.Square).then_inc(sq_done, 1)

            def rms(n):
                act.wait_ge(mean_done, n + 1)
                act.activation(mean[:], mean[:], ACT.Sqrt).then_inc(rms_done, 1)

            def up_pair(base, fbase, c, i, tail, n_norm=None):
                for j in (0, 1):
                    u = base + 2 * j
                    for v in (u + 2, u + 3):
                        split_hi(v, i, unit_width(v) if tail else KD * P)
                    if n_norm is not None and j == 0:
                        rms(n_norm)
                    act.wait_ge(acc_read[u % RING], reads(u, i) + 1)
                    act.activation(act_gate[:, j, :], gate[:, j, :], ACT.Silu).then_inc(silu_done, 1)
                    act.wait_ge(prod_done, 2 * i + (fbase + j + 1))
                    act.activation(hid_hi[:, 2 * i + (j + c), :], prod[:, j, :], ACT.Copy).then_inc(hid_hi_done, 1)

            def ffn(base, fb, n_norm, n_next):
                for c, (f0, n) in enumerate(CHUNKS):
                    u = chunk_base(base, c)
                    lastpair = 1 if c == len(CHUNKS) - 1 else 0
                    lo = 1 if c == 0 else 0
                    if lo:
                        up_pair(u, fb + f0, 0, 0, True, n_norm)
                    with act.Fori(lo, n // 2 - lastpair) as i:
                        up_pair(u, fb + f0, 0, i, False)
                    if lastpair:
                        i = n // 2 - 1
                        up_pair(u + 4 * i, fb + f0 + 2 * i, 2 * i, 0, True)
                    u += 2 * n
                    for m in range(KD):
                        if u + m + 2 < UNITS:
                            split_hi(u + m + 2, 0, unit_width(u + m + 2))
                        if c == len(CHUNKS) - 1:
                            act.wait_ge(acc_read[(u + m) % RING], reads(u + m, 0) + 1)
                            square(m, n_next)

            split_hi(0, 0, KD * P)
            for k in range(KD):
                act.wait_ge(x_loaded[k], 16)
                square(k, 0)
                if k == 3:
                    split_hi(1, 0, KD * P)
            act.preload_act_table_set("silu_and_others")
            ffn(FFN_A, 0, 0, 1)

            for kind, w in MIX_STEPS:
                if kind == "Ua":
                    split_hi(w + 2, 0, unit_width(w + 2))
                elif kind == "norm":
                    rms(w)
                    act.preload_act_table_set("natural_log_exp_and_others")
                elif kind == "Ub" and w >= GATE:
                    act.wait_ge(acc_read[w % RING], reads(w, 0) + 1)
                    act.wait_ge(hbias_made, 1)
                    act.activation(gsb[:, w - GATE, :], gsb[:, w - GATE, :], ACT.Tanh, scale=0.5,
                                   bias=hbias[:, 0, w - GATE:w - GATE + 1]).then_inc(gate_done, 1)
                elif kind == "fin":
                    what, pair, g = mix_kind(w)
                    n = w - MIX
                    if what in "qk":
                        act.wait_ge(raw_done, n + 1)
                        dst = (sq_hi if what == "q" else sk_hi)[:, pair % 2, :]
                        src = raw[:, w % 2, :]
                    elif what in ("rq", "rk"):
                        act.wait_ge(rope_step, 3 * (ROPES.index(w) + 1))
                        dst = dq_hi[pair][:, g, :] if what == "rq" else dk_hi[pair][:]
                        src = roped[:]
                    else:
                        act.wait_ge(turned, TURNED.index(w) + 1)
                        if what == "v":
                            dst = sv_hi[:, pair % 2, :, :]
                            src = acc[w % RING][:].rearrange("p (b c) -> p b c", b=BLK)
                        else:
                            dst = dv_hi[pair][:, :, 0:3:2, :]
                            src = acc[w % RING][:].rearrange("p (b h c) -> p b h c", b=BLK, h=2)
                    if what == "q" or what == "k":
                        if pair >= 2 and what == "q":
                            act.wait_ge(z_done, 3 * (2 * pair - 2))
                    if what == "v" and pair >= 2:
                        act.wait_ge(pv_done, 2 * pair - 2)
                    if what == "rq" and g == 0 and pair == 1:
                        act.wait_ge(pv_done, 2 * SB_PAIRS)
                    act.activation(dst, src, ACT.Copy).then_inc(op_hi_done, 1)
                elif kind == "scores":
                    for b in range(3):
                        t = 3 * w + b
                        e = ebuf[:, SB_AT[b]:SB_AT[b] + SB_WIDTH[b]]
                        act.wait_ge(z_done, t + 1)
                        if w:
                            act.wait_ge(a_split, 3 * (w - 1) + b + 1)
                        act.activation(e, bank[b][:, 0:SB_WIDTH[b]], ACT.Abs).then_inc(soft_step, 1)
                        act.wait_ge(soft_step, 3 * t + 1)
                        act.activation(e, e, ACT.Exp, scale=-1.0).then_inc(soft_step, 1)
                        act.wait_ge(soft_step, 3 * t + 2)
                        act.activation(e, e, ACT.Ln, bias=1.0).then_inc(soft_step, 1)
                elif kind == "suffix":
                    for b in range(3):
                        act.wait_ge(suffix_done, 3 * w + b + 1)
                        act.activation(ebuf[:, SB_AT[b]:SB_AT[b] + SB_WIDTH[b]], bank[b][:, 0:SB_WIDTH[b]],
                                       ACT.Exp).then_inc(a_done, 1)
                elif kind == "y":
                    rows = slice(HD * (w % 2), HD * (w % 2) + HD)
                    act.wait_ge(pv_done, w + 1)
                    act.activation(ys_hi[rows, w // 2, :], bank[3][rows, :], ACT.Copy).then_inc(ys_hi_done, 1)
                elif kind == "dscores":
                    n = DIL * w[0] + w[1]
                    act.wait_ge(max_step, 3 * (n + 1))
                    if n:
                        act.wait_ge(pt_turned, n)
                    for c, b, wd in ((0, 0, SEQ), (SEQ, 1, 2 * P)):
                        act.activation(prob[:, 0, c:c + wd], bank[b][:, 0:wd], ACT.Exp,
                                       bias=rmax[:, n % 2, 2:3], scale=HD ** -0.5).then_inc(p_done, 1)
                elif kind == "dturn":
                    j, r = w
                    n = DIL * j + r
                    act.wait_ge(pt_turned, n + 1)
                    if r == 0 and j:
                        act.wait_ge(dpv_done, j)
                    act.activation(pT_hi[:, :, r * P:(r + 1) * P], bank[2][:].rearrange("p (b c) -> p b c", b=DIL),
                                   ACT.Copy).then_inc(pt_hi_done, 1)
                elif kind == "dy":
                    rows = slice(HD * (w % 2), HD * (w % 2) + HD)
                    act.wait_ge(dy_step, 2 * w + 2)
                    act.activation(yd_hi[rows, w // 2, :], yraw[rows, :], ACT.Copy).then_inc(yd_hi_done, 1)

            for i in range(KD // 4):
                for j in range(12):
                    v = END + 12 * i + j + 2
                    split_hi(v, 0, unit_width(v))
                    m = 4 * i + j // 3
                    if j % 3 == 0:
                        act.wait_ge(acc_read[(END + j) % RING], reads(END + j, 3 * i) + 1)
                        act.activation(gdl[:, j // 3 % 2, :], gdl[:, j // 3 % 2, :], ACT.Tanh, scale=0.5,
                                       bias=hbias[:, 1, m:m + 1]).then_inc(gate_done, 1)
                    if j % 3 == 2:
                        act.wait_ge(merge_step, m + 1)
                        act.activation(mg_hi[:, m, :], part[:, 0, :], ACT.Copy, scale=0.5).then_inc(mg_hi_done, 1)
            for m in range(KD):
                split_hi(WO + m + 2, 0, KD * P)
                act.wait_ge(acc_read[(WO + m) % RING], reads(WO + m, 0) + 1)
                square(m, 2)
            act.preload_act_table_set("silu_and_others")
            ffn(FFN_B, NF, 2, 3)
            rms(3)

        @block.vector
        def _(dve):
            def split_lo(u0, i, width):
                s = u0 % RING
                dve.wait_ge(whi_done, 4 * i + (u0 + 1))
                if u0 >= RING:
                    dve.wait_ge(unit_done, 4 * i + (u0 - RING + 1))
                dve.tensor_tensor(w_lo[:, s, 0:width], w_raw[:, s, 0:width], w_hi[:, s, 0:width].bitcast(F32),
                                  ALU.subtract).then_inc(wlo_done, 1)

            def prep(m, n):
                g = gains[:, n, m:m + 1]
                dve.tensor_scalar(xg_hi[:, m, :], x[:, m, :], g, None, ALU.mult).then_inc(xg_hi_done, 1)
                dve.wait_ge(xg_hi_done, KD * n + m + 1)
                dve.scalar_tensor_tensor(xg_lo[:, m, :], x[:, m, :], g, xg_hi[:, m, :].bitcast(F32),
                                         ALU.mult, ALU.subtract).then_inc(xg_lo_done, 1)

            def add_square(m, n):
                if m:
                    dve.wait_ge(sq_done, KD * n + m + 1)
                    if m > 1:
                        dve.wait_ge(sum_done, (KD - 1) * n + m - 1)
                    dve.tensor_tensor(ssum[:], ssum[:], sq[:, m % 2, :], ALU.add).then_inc(sum_done, 1)

            def norm(n):
                dve.wait_ge(sumsq_done, n + 1)
                dve.tensor_scalar(mean[:], bank[0][:], 1.0 / D, EPS, ALU.mult, ALU.add).then_inc(mean_done, 1)
                dve.wait_ge(rms_done, n + 1)
                dve.reciprocal(rstd[:], mean[:]).then_inc(rstd_done, 1)
                dve.wait_ge(rstd_done, n + 1)

            def up_pair(base, fbase, c, i, tail, n_norm=None):
                for j in (0, 1):
                    u = base + 2 * j
                    for v in (u + 2, u + 3):
                        split_lo(v, i, unit_width(v) if tail else KD * P)
                    if n_norm is not None and j == 0:
                        norm(n_norm)
                    for t, dst in ((0, gate), (1, up)):
                        s = (u + t) % RING
                        dve.wait_ge(unit_done, 4 * i + (u + t + 1))
                        dve.tensor_tensor(dst[:, j, :], acc[s][:], rstd[:], ALU.mult).then_inc(acc_read[s], 1)
                    dve.wait_ge(silu_done, 2 * i + (fbase + j + 1))
                    dve.wait_ge(acc_read[s], reads(u + 1, i) + 1)
                    dve.tensor_tensor(prod[:, j, :], act_gate[:, j, :], up[:, j, :], ALU.mult).then_inc(prod_done, 1)
                    dve.wait_ge(hid_hi_done, 2 * i + (fbase + j + 1))
                    dve.tensor_tensor(hid_lo[:, 2 * i + (j + c), :], prod[:, j, :],
                                      hid_hi[:, 2 * i + (j + c), :].bitcast(F32), ALU.subtract).then_inc(hid_lo_done, 1)

            def update_x(u, m, scale):
                s = u % RING
                dve.wait_ge(unit_done, u + 1)
                dve.scalar_tensor_tensor(x[:, m, :], acc[s][:], scale, x[:, m, :], ALU.mult,
                                         ALU.add).then_inc(acc_read[s], 1)
                return s, reads(u, 0)

            def ffn(base, fb, n_norm, n_next):
                for c, (f0, n) in enumerate(CHUNKS):
                    u = chunk_base(base, c)
                    lastpair = 1 if c == len(CHUNKS) - 1 else 0
                    lo = 1 if c == 0 else 0
                    if lo:
                        up_pair(u, fb + f0, 0, 0, True, n_norm)
                    with dve.Fori(lo, n // 2 - lastpair) as i:
                        up_pair(u, fb + f0, 0, i, False)
                    if lastpair:
                        i = n // 2 - 1
                        up_pair(u + 4 * i, fb + f0 + 2 * i, 2 * i, 0, True)
                    u += 2 * n
                    for m in range(KD):
                        if u + m + 2 < UNITS:
                            split_lo(u + m + 2, 0, unit_width(u + m + 2))
                        s, before = update_x(u + m, m, 0.5)
                        if c == len(CHUNKS) - 1:
                            if n_next < 3:
                                dve.wait_ge(acc_read[s], before + 1)
                                prep(m, n_next)
                            add_square(m, n_next)

            def take_out(w):
                what, pair, g = mix_kind(w)
                if w - 2 >= MIX:
                    dve.wait_ge(op_lo_done, w - 2 - MIX + 1)
                dve.wait_ge(unit_done, w + 1)
                if what == "q":
                    dve.scalar_tensor_tensor(raw[:, w % 2, :], acc[w % RING][:], HD ** -0.5, rstd[:], ALU.mult,
                                             ALU.mult).then_inc(raw_done, 1)
                elif what == "rv":
                    dve.tensor_tensor(raw[:, w % 2, :].rearrange("c (r p) -> c p r", r=DIL),
                                      acc[w % RING][:].rearrange("c (p r) -> c p r", r=DIL),
                                      rstd[:].rearrange("c (p r) -> c p r", r=DIL), ALU.mult).then_inc(raw_done, 1)
                else:
                    dve.tensor_tensor(raw[:, w % 2, :], acc[w % RING][:], rstd[:], ALU.mult).then_inc(raw_done, 1)

            dve.memset(ones[:], 1.0).then_inc(consts_made, 1)
            dve.wait_ge(gains_loaded, 16)
            split_lo(0, 0, KD * P)
            for k in range(KD):
                dve.wait_ge(x_loaded[k], 16)
                prep(k, 0)
                add_square(k, 0)
                if k == 3:
                    split_lo(1, 0, KD * P)
            dve.wait_ge(const_loaded, 16 * N_CONST)
            dve.tensor_scalar(hbias[:], bias[:], 0.5, None, ALU.mult).then_inc(hbias_made, 1)
            dve.memset(negones[:].bitcast(F32), -1.0).then_inc(consts_made, 1)
            dve.tensor_copy(tri[:], trif).then_inc(consts_made, 1)
            dve.wait_ge(consts_made, 3)
            ffn(FFN_A, 0, 0, 1)

            heads_out = 0
            for kind, w in MIX_STEPS:
                if kind == "Ua":
                    split_lo(w + 2, 0, unit_width(w + 2))
                elif kind == "norm":
                    norm(w)
                    take_out(MIX)
                elif kind == "Ub" and w >= GATE:
                    dve.wait_ge(unit_done, w + 1)
                    dve.wait_ge(dpv_done, 2)
                    dve.tensor_tensor(gsb[:, w - GATE, :], acc[w % RING][:], rstd[:],
                                      ALU.mult).then_inc(acc_read[w % RING], 1)
                elif kind == "Ub":
                    if w != MIX:
                        take_out(w)
                elif kind == "fin":
                    what, pair, g = mix_kind(w)
                    n = w - MIX
                    fin = n + 1
                    src = raw[:, w % 2, :]
                    if what in "qk":
                        hi, lo = (sq_hi, sq_lo) if what == "q" else (sk_hi, sk_lo)
                        dve.wait_ge(op_hi_done, fin)
                        dve.tensor_tensor(lo[:, pair % 2, :], src, hi[:, pair % 2, :].bitcast(F32),
                                          ALU.subtract).then_inc(op_lo_done, 1)
                    elif what in ("rq", "rk"):
                        t = 3 * ROPES.index(w)
                        if t:
                            dve.wait_ge(op_lo_done, n)
                        if heads_out:
                            dve.wait_ge(yd_done, heads_out)
                        dve.tensor_tensor(rope1[:], src, cos[:], ALU.mult).then_inc(rope_step, 1)
                        dve.wait_ge(turned, TURNED.index(w) + 1)
                        dve.tensor_tensor(rope2[:], acc[w % RING][:], sin[:], ALU.mult).then_inc(rope_step, 1)
                        dve.wait_ge(rope_step, t + 2)
                        dve.tensor_tensor(roped[:].rearrange("c (r p) -> c p r", r=DIL),
                                          rope1[:].rearrange("c (p r) -> c p r", r=DIL),
                                          rope2[:].rearrange("c (p r) -> c p r", r=DIL),
                                          ALU.add).then_inc(rope_step, 1)
                        hi = dq_hi[pair][:, g, :] if what == "rq" else dk_hi[pair][:]
                        lo = dq_lo[pair][:, g, :] if what == "rq" else dk_lo[pair][:]
                        dve.wait_ge(rope_step, t + 3)
                        dve.wait_ge(op_hi_done, fin)
                        dve.tensor_tensor(lo, roped[:], hi.bitcast(F32), ALU.subtract).then_inc(op_lo_done, 1)
                    elif what == "v":
                        dve.wait_ge(op_hi_done, fin)
                        dve.tensor_tensor(sv_lo[:, pair % 2, :, :],
                                          acc[w % RING][:].rearrange("p (b c) -> p b c", b=BLK),
                                          sv_hi[:, pair % 2, :, :].bitcast(F32), ALU.subtract).then_inc(op_lo_done, 1)
                    else:
                        dve.wait_ge(op_hi_done, fin)
                        dve.tensor_tensor(dv_lo[pair][:, :, 0:3:2, :],
                                          acc[w % RING][:].rearrange("p (b h c) -> p b h c", b=BLK, h=2),
                                          dv_hi[pair][:, :, 0:3:2, :].bitcast(F32), ALU.subtract).then_inc(op_lo_done, 1)
                elif kind == "scores":
                    for b in range(3):
                        t = 3 * w + b
                        cols = slice(SB_AT[b], SB_AT[b] + SB_WIDTH[b])
                        dve.wait_ge(soft_step, 3 * t + 3)
                        dve.scalar_tensor_tensor(ebuf[:, cols], bank[b][:, 0:SB_WIDTH[b]], 0.0, ebuf[:, cols],
                                                 ALU.max, ALU.add).then_inc(sp_step, 1)
                        dve.wait_ge(sp_step, 2 * t + 1)
                        if w:
                            dve.wait_ge(pv_done, w)
                        dve.tensor_copy(spA_hi[:, cols], ebuf[:, cols]).then_inc(sp_step, 1)
                        dve.wait_ge(sp_step, 2 * t + 2)
                        dve.tensor_tensor(spA_lo[:, cols], ebuf[:, cols], spA_hi[:, cols].bitcast(F32),
                                          ALU.subtract).then_inc(sp_split, 1)
                elif kind == "suffix":
                    for b in range(3):
                        t = 3 * w + b
                        cols = slice(SB_AT[b], SB_AT[b] + SB_WIDTH[b])
                        dve.wait_ge(a_done, t + 1)
                        dve.wait_ge(suffix_done, 3 * w + 3)
                        dve.tensor_copy(spA_hi[:, cols], ebuf[:, cols]).then_inc(a_hi_done, 1)
                        dve.wait_ge(a_hi_done, t + 1)
                        dve.tensor_tensor(spA_lo[:, cols], ebuf[:, cols], spA_hi[:, cols].bitcast(F32),
                                          ALU.subtract).then_inc(a_split, 1)
                elif kind == "y":
                    rows = slice(HD * (w % 2), HD * (w % 2) + HD)
                    dve.wait_ge(ys_hi_done, w + 1)
                    dve.tensor_tensor(ys_lo[rows, w // 2, :], bank[3][rows, :], ys_hi[rows, w // 2, :].bitcast(F32),
                                      ALU.subtract).then_inc(ys_done, 1)
                elif kind == "dscores":
                    j, r = w
                    n = DIL * j + r
                    t = rmax[:, n % 2, :]
                    dve.wait_ge(ds_done, n + 1)
                    dve.tensor_reduce(t[:, 0:1], bank[0][:], AX.X, ALU.max).then_inc(max_step, 1)
                    dve.tensor_reduce(t[:, 1:2], bank[1][:, 0:2 * P], AX.X, ALU.max).then_inc(max_step, 1)
                    dve.wait_ge(max_step, 3 * n + 2)
                    dve.tensor_scalar(t[:, 2:3], t[:, 0:1], t[:, 1:2], -HD ** -0.5, ALU.max,
                                      ALU.mult).then_inc(max_step, 1)
                    own = prob[:, 0, r * P:(r + 1) * P]
                    dve.wait_ge(p_done, 2 * n + 2)
                    dve.tensor_tensor(own, own, prob[:, 0, SEQ:SEQ + P], ALU.add).then_inc(psum_step, 1)
                    dve.wait_ge(psum_step, 2 * n + 1)
                    dve.tensor_tensor(own, own, prob[:, 0, SEQ + P:SEQ + 2 * P], ALU.add).then_inc(psum_step, 1)
                elif kind == "dturn":
                    j, r = w
                    n = DIL * j + r
                    dve.wait_ge(pt_hi_done, n + 1)
                    dve.tensor_tensor(pT_lo[:, :, r * P:(r + 1) * P], bank[2][:].rearrange("p (b c) -> p b c", b=DIL),
                                      pT_hi[:, :, r * P:(r + 1) * P].bitcast(F32), ALU.subtract).then_inc(pt_split, 1)
                elif kind == "dy":
                    rows = slice(HD * (w % 2), HD * (w % 2) + HD)
                    if w:
                        dve.wait_ge(yd_done, w)
                    heads_out = w + 1
                    dve.wait_ge(dpv_done, w + 1)
                    other = slice(HD * (1 - w % 2), HD * (1 - w % 2) + HD)
                    dve.reciprocal(rden[rows, :], bank[3][other, :]).then_inc(dy_step, 1)
                    dve.wait_ge(dy_step, 2 * w + 1)
                    dve.tensor_tensor(yraw[rows, :].rearrange("c (p r) -> c r p", r=DIL),
                                      bank[3][rows, :].rearrange("c (r p) -> c r p", r=DIL),
                                      rden[rows, :].rearrange("c (r p) -> c r p", r=DIL), ALU.mult).then_inc(dy_step, 1)
                    dve.wait_ge(dy_step, 2 * w + 2)
                    dve.wait_ge(yd_hi_done, w + 1)
                    dve.tensor_tensor(yd_lo[rows, w // 2, :], yraw[rows, :], yd_hi[rows, w // 2, :].bitcast(F32),
                                      ALU.subtract).then_inc(yd_done, 1)

            for i in range(KD // 4):
                for j in range(12):
                    u, v = END + j, END + 12 * i + j + 2
                    s = u % RING
                    m = 4 * i + j // 3
                    split_lo(v, 0, unit_width(v))
                    dve.wait_ge(unit_done, 12 * i + (u + 1))
                    if j % 3 == 0:
                        dve.tensor_tensor(gdl[:, j // 3 % 2, :], acc[s][:], rstd[:], ALU.mult).then_inc(acc_read[s], 1)
                    elif j % 3 == 1:
                        if m:
                            dve.wait_ge(mg_lo_done, m)
                        dve.scalar_tensor_tensor(part[:, 0, :], gsb[:, m, :], 1.0, acc[s][:], ALU.add,
                                                 ALU.mult).then_inc(acc_read[s], 1)
                    else:
                        dve.wait_ge(gate_done, m + (KD + 1))
                        dve.scalar_tensor_tensor(part[:, 1, :], gdl[:, j // 3 % 2, :], 1.0, acc[s][:], ALU.add,
                                                 ALU.mult).then_inc(acc_read[s], 1)
                        dve.wait_ge(acc_read[s], reads(u, 3 * i) + 1)
                        dve.wait_ge(acc_read[(u - 1) % RING], reads(u - 1, 3 * i) + 1)
                        dve.tensor_tensor(part[:, 0, :], part[:, 0, :], part[:, 1, :], ALU.add).then_inc(merge_step, 1)
                        dve.wait_ge(merge_step, m + 1)
                        dve.wait_ge(mg_hi_done, m + 1)
                        dve.scalar_tensor_tensor(mg_lo[:, m, :], part[:, 0, :], 0.5, mg_hi[:, m, :].bitcast(F32),
                                                 ALU.mult, ALU.subtract).then_inc(mg_lo_done, 1)
            for m in range(KD):
                split_lo(WO + m + 2, 0, KD * P)
                s, before = update_x(WO + m, m, 1.0)
                dve.wait_ge(acc_read[s], before + 1)
                prep(m, 2)
                add_square(m, 2)
            ffn(FFN_B, NF, 2, 3)
            norm(3)
            for m in range(KD):
                dve.scalar_tensor_tensor(x[:, m, :], x[:, m, :], gains[:, 3, m:m + 1], rstd[:], ALU.mult,
                                         ALU.mult).then_inc(y_ready, 1)

        @block.gpsimd
        def _(pool):
            for jp in range(DL_PAIRS):
                if jp == 0:
                    pool.wait_ge(raw_done, 1)
                else:
                    pool.wait_ge(pv_done, 2 * SB_PAIRS)
                pool.memset(dv_hi[jp][:, :, 1, :].bitcast(F32), 1.0).then_inc(dv_ones, 1)
                pool.memset(dv_lo[jp][:, :, 1, :].bitcast(F32), 0.0).then_inc(dv_ones, 1)

        @block.tensor
        def _(pe):
            def product(o, w_h, w_l, r_h, r_l, first, last, check=False):
                pe.matmul(o, w_h, r_h, start=first, stop=False, skip_group_check=check)
                pe.matmul(o, w_h, r_l, start=False, stop=False, skip_group_check=check)
                return pe.matmul(o, w_l, r_h, start=False, stop=last, skip_group_check=check)

            def bank_free(u0, i):
                last = u0 - RING
                if last < 0:
                    return
                if not MIX <= last < GATE:
                    pe.wait_ge(acc_read[u0 % RING], reads(u0, i))
                    return
                kind = mix_kind(last)[0]
                if kind in ("q", "k"):
                    pe.wait_ge(raw_done, last - MIX + 1)
                elif kind in ("rq", "rk"):
                    pe.wait_ge(rope_step, 3 * ROPES.index(last) + 2)
                else:
                    pe.wait_ge(op_lo_done, last - MIX + 1)

            def unit(u0, i, rhs, ks, before=None, half=None):
                s = u0 % RING
                n = len(ks)
                lo, hi = {None: (0, n), 0: (0, n // 2), 1: (n // 2, n)}[half]
                if half != 1:
                    pe.wait_ge(wlo_done, 4 * i + (u0 + 1))
                    bank_free(u0, i)
                for k in range(lo, hi):
                    if before:
                        before(k)
                    r_h, r_l = rhs(ks[k])
                    mm = product(acc[s][:], w_hi[:, s, k * P:(k + 1) * P], w_lo[:, s, k * P:(k + 1) * P], r_h, r_l,
                                 k == 0, k == n - 1)
                if half != 0:
                    mm.then_inc(unit_done, 1)

            xg = lambda k: (xg_hi[:, k, :], xg_lo[:, k, :])
            hid = lambda k: (hid_hi[:, k, :], hid_lo[:, k, :])
            K8 = list(range(KD))

            def norm(n):
                pe.wait_ge(sum_done, (KD - 1) * (n + 1))
                pe.matmul(bank[0][:], ones[:], ssum[:], start=True, stop=True).then_inc(sumsq_done, 1)

            def ffn(base, fb, n_norm):
                for c, (f0, n) in enumerate(CHUNKS):
                    u = chunk_base(base, c)
                    lo = 0
                    if c == 0:
                        lo = 1
                        unit(u, 0, xg, K8, lambda k: pe.wait_ge(xg_lo_done, KD * n_norm + k + 1))
                        norm(n_norm)
                        for j in (1, 2, 3):
                            unit(u + j, 0, xg, K8)
                    with pe.Fori(lo, n // 2) as i:
                        for j in range(4):
                            unit(u + j, i, xg, K8)
                    u += 2 * n
                    ks = list(range(n))
                    for m in range(4):
                        unit(u + m, 0, hid, ks, (lambda k: pe.wait_ge(hid_lo_done, fb + f0 + k + 1)) if m == 0 else None)
                    for m in range(4, 8):
                        unit(u + m, 0, hid, ks)

            pe.wait_ge(consts_made, 1)
            ffn(FFN_A, 0, 0)

            for kind, w in MIX_STEPS:
                if kind == "Ua":
                    unit(w, 0, xg, K8, (lambda k: pe.wait_ge(xg_lo_done, KD + k + 1)) if w == MIX else None, half=0)
                elif kind == "Ub":
                    unit(w, 0, xg, K8, (lambda k: pe.wait_ge(xg_lo_done, KD + k + 1)) if w == MIX else None, half=1)
                elif kind == "norm":
                    norm(w)
                elif kind == "fin":
                    what, pair, g = mix_kind(w)
                    if what in "qk":
                        continue
                    pe.wait_ge(raw_done, w - MIX + 1)
                    if what in ("rq", "rk"):
                        pe.matmul(acc[w % RING][:], rot[:], raw[:, w % 2, :], start=True, stop=True).then_inc(turned, 1)
                    else:
                        for b in range(BLK):
                            mm = pe.transpose(acc[w % RING][:, b * P:(b + 1) * P], raw[:, w % 2, b * P:(b + 1) * P],
                                              identf[:])
                        mm.then_inc(turned, 1)
                elif kind == "scores":
                    hp, a = w // 2, w % 2
                    rows = slice(HD * a, HD * a + HD)
                    pe.wait_ge(op_lo_done, 3 * hp + 2)
                    if w == 0:
                        pe.wait_ge(mean_done, 2)
                        pe.wait_ge(consts_made, 3)
                        pe.wait_ge(const_loaded, 16 * N_CONST)
                    for b, parts in enumerate(SB_BANKS):
                        if w:
                            pe.wait_ge(a_done, 3 * (w - 1) + b + 1)
                        for n, (i, col) in enumerate(parts):
                            o = bank[b][:, col:col + SEQ - P * i]
                            ks = slice(P * i, P * i + P)
                            product(o, sk_hi[rows, hp % 2, ks], sk_lo[rows, hp % 2, ks],
                                    sq_hi[rows, hp % 2, P * i:SEQ], sq_lo[rows, hp % 2, P * i:SEQ],
                                    n == 0, False, True)
                        for i, col in parts:
                            mm = pe.matmul(bank[b][:, col:col + P], identb[:], mask_sb[:], start=False, stop=False,
                                           skip_group_check=True)
                        mm.then_inc(z_done, 1)
                elif kind == "suffix":
                    for b, parts in enumerate(SB_BANKS):
                        need = (2, 2, 3)[b]
                        pe.wait_ge(sp_split, 3 * w + need)
                        for i, col in parts:
                            for j in range(i, BLK):
                                bj, cj = sb_block(j)
                                at = slice(SB_AT[bj] + cj, SB_AT[bj] + cj + SEQ - P * j)
                                o = bank[b][:, col + P * (j - i):col + SEQ - P * i]
                                m = tri if i == j else negones
                                pe.matmul(o, m[:], spA_hi[:, at], start=False, stop=False, skip_group_check=True)
                                mm = pe.matmul(o, m[:], spA_lo[:, at], start=False, stop=True, skip_group_check=True)
                        mm.then_inc(suffix_done, 1)
                elif kind == "pv":
                    hp = w // 2
                    pe.wait_ge(op_lo_done, 3 * hp + 3)
                    pe.wait_ge(a_split, 3 * w + 3)
                    if w:
                        pe.wait_ge(ys_done, w)
                    for i in range(BLK):
                        b, col = sb_block(i)
                        at = slice(SB_AT[b] + col, SB_AT[b] + col + SEQ - P * i)
                        mm = product(bank[3][:, P * i:SEQ], sv_hi[:, hp % 2, i, :], sv_lo[:, hp % 2, i, :],
                                     spA_hi[:, at], spA_lo[:, at], i == 0, i == BLK - 1, True)
                    mm.then_inc(pv_done, 1)
                elif kind == "dscores":
                    j, r = w
                    jp, n = j // 2, DIL * j + r
                    rows = slice(HD * (j % 2), HD * (j % 2) + HD)
                    own = slice(r * P, (r + 1) * P)
                    pe.wait_ge(op_lo_done, 3 * SB_PAIRS + (NG + 2) * jp + NG + 1)
                    if n:
                        pe.wait_ge(p_done, 2 * n)
                    else:
                        pe.wait_ge(a_done, 6 * SB_PAIRS)
                    product(bank[0][:], dq_hi[jp][rows, 0, own], dq_lo[jp][rows, 0, own], dk_hi[jp][rows, :],
                            dk_lo[jp][rows, :], True, False, True)
                    for g in (1, 2):
                        product(bank[1][:, (g - 1) * P:g * P], dq_hi[jp][rows, g, own], dq_lo[jp][rows, g, own],
                                dk_hi[jp][rows, own], dk_lo[jp][rows, own], g == 1, False, True)
                    pe.matmul(bank[0][:], identb[:], mask_g0[:, r, :], start=False, stop=True, skip_group_check=True)
                    pe.matmul(bank[1][:, 0:2 * P], identb[:], mask_g12[:], start=False, stop=True,
                              skip_group_check=True).then_inc(ds_done, 1)
                elif kind == "dturn":
                    j, r = w
                    n = DIL * j + r
                    pe.wait_ge(psum_step, 2 * n + 2)
                    if n:
                        pe.wait_ge(pt_split, n)
                    for b in range(DIL):
                        mm = pe.transpose(bank[2][:, b * P:(b + 1) * P], prob[:, 0, b * P:(b + 1) * P], identf[:])
                    mm.then_inc(pt_turned, 1)
                elif kind == "dpv":
                    jp = w // 2
                    pe.wait_ge(op_lo_done, 3 * SB_PAIRS + (NG + 2) * (jp + 1))
                    pe.wait_ge(pt_split, DIL * (w + 1))
                    pe.wait_ge(dv_ones, 2 * (jp + 1))
                    if w:
                        pe.wait_ge(yd_done, w)
                    else:
                        pe.wait_ge(ys_done, 2 * SB_PAIRS)
                    for b in range(DIL):
                        h = slice(w % 2, w % 2 + 2)
                        mm = product(bank[3][:], dv_hi[jp][:, b, h, :], dv_lo[jp][:, b, h, :],
                                     pT_hi[:, b, :], pT_lo[:, b, :], b == 0, b == DIL - 1)
                    mm.then_inc(dpv_done, 1)

            pe.wait_ge(yd_done, 2 * DL_PAIRS)
            ys = lambda k: (ys_hi[:, k, :], ys_lo[:, k, :])
            yd = lambda k: (yd_hi[:, k, :], yd_lo[:, k, :])
            with pe.Fori(0, KD // 4) as i:
                for j in range(0, 12, 3):
                    unit(END + j, 3 * i, xg, K8)
                    unit(END + j + 1, 3 * i, ys, K8[0:SB_PAIRS])
                    unit(END + j + 2, 3 * i, yd, K8[0:DL_PAIRS])
            for m in range(KD):
                unit(WO + m, 0, lambda k: (mg_hi[:, k, :], mg_lo[:, k, :]), K8,
                     (lambda k: pe.wait_ge(mg_lo_done, k + 1)) if m == 0 else None)
            ffn(FFN_B, NF, 2)
            norm(3)


def constants():
    half = HD // 2
    inv = (np.float32(10000.0) ** (-np.arange(half, dtype=np.float32) / np.float32(half))).astype(np.float32)
    ang = (np.arange(SEQ, dtype=np.float32)[:, None] * inv[None, :]).astype(np.float32).T
    row = np.arange(P) % half
    d = np.arange(P)
    rot = np.zeros((P, P), np.float32)
    low = d % HD < half
    rot[d[low] + half, d[low]] = -1.0
    rot[d[~low] - half, d[~low]] = 1.0
    i = np.arange(P)
    t = DIL * i[:, None, None, None] + np.arange(DIL)[None, :, None, None]
    s = DIL * i[None, None, None, :] + np.arange(DIL)[None, None, :, None]
    ok0 = (t - s >= 0) & (t - s <= P)
    back = i[:, None] - i[None, :]
    ok12 = np.concatenate([back >= 0, (back >= 0) & (back % 4 == 0)], 1)

    def bf16_bits(v):
        return (np.asarray(v, np.float32).view(np.uint32) >> 16).astype(np.uint16)

    return {
        "cos": np.cos(ang.astype(np.float64)).astype(np.float32)[row],
        "sin": np.sin(ang.astype(np.float64)).astype(np.float32)[row],
        "rot": rot,
        "identf": np.eye(P, dtype=np.float32),
        "trif": -(i[:, None] >= i[None, :]).astype(np.float32),
        "identb": bf16_bits(np.eye(P)),
        "mask_sb": bf16_bits(np.where(i[:, None] < i[None, :], 0.0, NEG)),
        "mask_g0": bf16_bits(np.where(ok0, 0.0, NEG)).reshape(P, DIL, SEQ),
        "mask_g12": bf16_bits(np.where(ok12, 0.0, NEG)),
    }


def kernel(**inputs):
    import concourse.bacc as bacc
    from concourse.bass_utils import run_bass_kernel_spmd

    a = {k: np.asarray(v) for k, v in inputs.items()}

    def units(w):
        k, m = w.shape
        return w.reshape(k // P, P, m // P, P).transpose(2, 1, 0, 3).reshape(m // P, P, k)

    def pairs(w1, w3):
        return np.stack([units(w1), units(w3)], 1).reshape(2 * NF, P, D)

    win = units(a["w_in"][0])
    SBT, DQT = SB_PAIRS, NG * DL_PAIRS
    order = []
    for hp in range(SB_PAIRS):
        order += [hp, SBT + hp, 2 * SBT + hp]
    dq, dk = 3 * SBT, 3 * SBT + DQT
    for jp in range(DL_PAIRS):
        order += [dq + DL_PAIRS * g + jp for g in range(NG)] + [dk + jp, dk + DL_PAIRS + jp]
    gate0 = dk + 2 * DL_PAIRS
    wend = np.concatenate([win[gate0 + KD:gate0 + 2 * KD], units(a["w_sb_out"][0]),
                           units(a["w_dil_out"][0])], 2)
    cols = lambda v: v.reshape(-1, P).T
    arrays = {
        "xT": a["x"][0].T.reshape(KD, P, SEQ).transpose(1, 0, 2),
        "gains": np.stack([cols(a[n].reshape(-1)) for n in ("g_ffn1", "g_mix", "g_ffn2", "g_final")], 1),
        "bias": cols(a["b_gate"][0]).reshape(P, 2, KD),
        "w13a": pairs(a["w1_a"][0], a["w3_a"][0]), "w2a": units(a["w2_a"][0]),
        "w13b": pairs(a["w1_b"][0], a["w3_b"][0]), "w2b": units(a["w2_b"][0]),
        "wmix": win[order], "wgate": win[gate0:gate0 + KD], "wend": wend, "wo": units(a["w_o"][0]),
    }
    arrays.update(constants())
    arrays = {k: np.ascontiguousarray(v) for k, v in arrays.items()}

    nc = bacc.Bacc("TRN2", target_bir_lowering=False, num_devices=1)
    A = {n: nc.dram_tensor("in_" + n, v.shape, mybir.dt.from_np(v.dtype), kind="ExternalInput").ap()
         for n, v in arrays.items()}
    out = nc.dram_tensor("out", (P, KD, SEQ), mybir.dt.float32, kind="ExternalOutput").ap()
    build(nc, A, out)
    r = run_bass_kernel_spmd(nc, [{"in_" + n: v for n, v in arrays.items()}], core_ids=[0])
    y = r.results[0]["out"]
    return np.ascontiguousarray(y.transpose(1, 0, 2).reshape(1, D, SEQ).transpose(0, 2, 1))
```

```python
from contextlib import ExitStack

import numpy as np

import concourse.bass as bass
from concourse import mybir

P = 128
SEQ = 512
D = 1024
KD = D // P
FF = 2816
NF = FF // P
CHUNKS = ((0, 8), (8, 8), (16, 6))
HD = 64
SB_PAIRS = 4
DL_PAIRS = 2
NG = 3
DIL = 4
BLK = SEQ // P
EPS = 1e-6
NEG = -1e30
RING = 4

FFN_UNITS = 3 * NF + 2
FFN_A = 0
MIX = 2 * NF + len(CHUNKS) * KD
MIX_UNITS = 3 * SB_PAIRS + (NG + 2) * DL_PAIRS
GATE = MIX + MIX_UNITS
END = GATE + KD
WO = END + 3 * KD
FFN_B = WO + KD
UNITS = FFN_B + 2 * NF + len(CHUNKS) * KD
DL_FILL = (2, 1, 2, 1, 2, 1, 2, 2, 1, 2, 1, 2, 1, 2, 1, 2)
END_COLS = ((0, 1024), (1024, 512), (1536, 256))
SB_BANKS = (((1, 0), (3, 384)), ((2, 0),), ((0, 0),))
SB_WIDTH = (512, 256, 512)
SB_AT = (0, 512, 768)


def chunk_base(base, c):
    return base + sum(2 * n + KD for _, n in CHUNKS[:c])


def unit_width(u):
    for base in (FFN_A, FFN_B):
        for c, (_, n) in enumerate(CHUNKS):
            at = chunk_base(base, c) + 2 * n
            if at <= u < at + KD:
                return n * P
    if END <= u < WO:
        return END_COLS[(u - END) % 3][1]
    return KD * P


def sb_block(i):
    for b, parts in enumerate(SB_BANKS):
        for blk, col in parts:
            if blk == i:
                return b, col


def mix_schedule():
    s = []
    held = []
    halves = [(half, u) for u in range(MIX, END) for half in ("Ua", "Ub")]

    def fill(n):
        for _ in range(n):
            half, u = halves.pop(0)
            s.append((half, u))
            if half == "Ua" and MIX < u <= GATE:
                s.append(("fin", u - 1))
            if half == "Ub" and u >= GATE:
                held.append(u)
        if ("dpv", 1) in s:
            while held:
                s.append(("gate", held.pop(0)))

    fill(2)
    s.append(("norm", 1))
    fill(4)
    s.append(("scores", 0))
    for h in range(2 * SB_PAIRS):
        wide = h // 2 == SB_PAIRS - 1
        fill(3 if wide else 2)
        if h:
            s.append(("y", h - 1))
        s.append(("suffix", h))
        fill(2 if wide else 1)
        s.append(("scores", h + 1) if h + 1 < 2 * SB_PAIRS else ("dscores", (0, 0)))
        s.append(("pv", h))
    blocks = [(j, r) for j in range(2 * DL_PAIRS) for r in range(DIL)]
    for n, (j, r) in enumerate(blocks):
        fill(DL_FILL[n] - 1)
        if n == 0:
            s.append(("y", 2 * SB_PAIRS - 1))
        if n + 1 < len(blocks):
            s.append(("dscores", blocks[n + 1]))
        s.append(("dadd", (j, r)))
        fill(1)
        if r == 0 and j:
            s.append(("dpv", j - 1))
        s.append(("dturn", (j, r)))
        s.append(("dlo", (j, r)))
        if r == 0 and j:
            s.append(("dy", j - 1))
    s.append(("dpv", 2 * DL_PAIRS - 1))
    fill(len(halves))
    s.append(("dy", 2 * DL_PAIRS - 1))
    return s


MIX_STEPS = mix_schedule()
FINS = [w for kind, w in MIX_STEPS if kind == "fin"]


def mix_kind(u):
    n = u - MIX
    if n < 3 * SB_PAIRS:
        return ("q", "k", "v")[n % 3], n // 3, 0
    n -= 3 * SB_PAIRS
    g = n % (NG + 2)
    return ("rq" if g < NG else ("rk", "rv")[g - NG]), n // (NG + 2), min(g, NG - 1)


ROPES = [u for u in FINS if mix_kind(u)[0] in ("rq", "rk")]
TURNED = [u for u in FINS if mix_kind(u)[0] not in ("q", "k")]


def build(nc, A, out):
    F32, F32R, BF16 = mybir.dt.float32, mybir.dt.float32r, mybir.dt.bfloat16
    ALU, ACT, AX = mybir.AluOpType, mybir.ActivationFunctionType, mybir.AxisListType
    ctx = ExitStack()
    with ctx:
        def sb(name, shape, dt=F32, where=ctx):
            return where.enter_context(nc.sbuf_tensor(name, shape, dt))

        def sem(name):
            return ctx.enter_context(nc.semaphore(name))

        x = sb("x", [P, KD, SEQ])
        xg_hi = sb("xg_hi", [P, KD, SEQ], F32R)
        xg_lo = sb("xg_lo", [P, KD, SEQ], F32R)
        w_raw = sb("w_raw", [P, RING, KD * P])
        w_hi = sb("w_hi", [P, RING, KD * P], F32R)
        w_lo = sb("w_lo", [P, RING, KD * P], F32R)
        rstd = sb("rstd", [P, SEQ])
        gains = sb("gains", [P, 4, KD])
        bias = sb("bias", [P, 2, KD])
        hbias = sb("hbias", [P, 2, KD])
        ones = sb("ones", [P, P])
        cos = sb("cos", [P, SEQ])
        sin = sb("sin", [P, SEQ])
        rot = sb("rot", [P, P])
        identf = sb("identf", [P, P])
        tri = sb("tri", [P, P], F32R)
        negones = sb("negones", [P, P], F32R)
        identb = sb("identb", [P, P], BF16)
        mask_sb = sb("mask_sb", [P, P], BF16)
        mask_g0 = sb("mask_g0", [P, DIL, SEQ], BF16)
        mask_g12 = sb("mask_g12", [P, 2 * P], BF16)
        rope1 = sb("rope1", [P, SEQ])
        rope2 = sb("rope2", [P, SEQ])
        roped = sb("roped", [P, SEQ])
        stats = sb("stats", [P, 2, 4])
        mean = rope1

        with ExitStack() as ffn:
            ssum = sb("ssum", [P, SEQ], F32, ffn)
            sq = sb("sq", [P, 2, SEQ], F32, ffn)
            hid_hi = sb("hid_hi", [P, 8, SEQ], F32R, ffn)
            hid_lo = sb("hid_lo", [P, 8, SEQ], F32R, ffn)
            gate = sb("gate", [P, 2, SEQ], F32, ffn)
            act_gate = sb("act_gate", [P, 2, SEQ], F32, ffn)
            up = sb("up", [P, 2, SEQ], F32, ffn)
            prod = sb("prod", [P, 2, SEQ], F32, ffn)
            trif = prod[:, 1, 0:P]
        with ExitStack() as mix:
            ys_hi = sb("ys_hi", [P, SB_PAIRS, SEQ], F32R, mix)
            ys_lo = sb("ys_lo", [P, SB_PAIRS, SEQ], F32R, mix)
            yd_hi = sb("yd_hi", [P, DL_PAIRS, SEQ], F32R, mix)
            yd_lo = sb("yd_lo", [P, DL_PAIRS, SEQ], F32R, mix)
            with ExitStack() as att:
                raw = sb("raw", [P, 2, SEQ], F32, att)
                with ExitStack() as s:
                    spA_hi = sb("spA_hi", [P, 1280], F32R, s)
                    spA_lo = sb("spA_lo", [P, 1280], F32R, s)
                    ebuf = sb("ebuf", [P, 1280], F32, s)
                    sv_lo = sb("sv_lo", [P, 2, BLK, P], F32R, s)
                pT_hi = sb("pT_hi", [P, DIL, SEQ], F32R, att)
                pT_lo = sb("pT_lo", [P, DIL, SEQ], F32R, att)
                prob = sb("prob", [P, 2, 6 * P], F32, att)
                dq_hi = [None, None]
                dq_lo, dk_hi, dk_lo, dv_hi, dv_lo = ([None, None] for _ in range(5))

                def dl_buffers(jp, where):
                    dq_hi[jp] = sb(f"dq_hi{jp}", [P, NG, SEQ], F32R, where)
                    dq_lo[jp] = sb(f"dq_lo{jp}", [P, NG, SEQ], F32R, where)
                    dk_hi[jp] = sb(f"dk_hi{jp}", [P, SEQ], F32R, where)
                    dk_lo[jp] = sb(f"dk_lo{jp}", [P, SEQ], F32R, where)
                    dv_hi[jp] = sb(f"dv_hi{jp}", [P, DIL, P], F32R, where)
                    dv_lo[jp] = sb(f"dv_lo{jp}", [P, DIL, P], F32R, where)
                with ExitStack() as s:
                    sq_hi = sb("sq_hi", [P, 2, SEQ], F32R, s)
                    sq_lo = sb("sq_lo", [P, 2, SEQ], F32R, s)
                    sk_hi = sb("sk_hi", [P, 2, SEQ], F32R, s)
                    sk_lo = sb("sk_lo", [P, 2, SEQ], F32R, s)
                    sv_hi = sb("sv_hi", [P, 2, BLK, P], F32R, s)
                dl_buffers(1, att)
                with ExitStack() as s:
                    dl_buffers(0, s)
                gsb = sb("gsb", [P, KD, SEQ], F32, att)
            with ExitStack() as end:
                mg_hi = sb("mg_hi", [P, KD, SEQ], F32R, end)
                mg_lo = sb("mg_lo", [P, KD, SEQ], F32R, end)
                gdl = sb("gdl", [P, 2, SEQ], F32, end)
                part = sb("part", [P, 2, SEQ], F32, end)

        acc = [ctx.enter_context(nc.psum_tensor(f"acc{i}", [P, SEQ], F32)) for i in range(RING)]
        pair_bank = ctx.enter_context(nc.psum_tensor("pair_bank", [P, 2 * SEQ], F32))
        bank = [pair_bank[:, 0:SEQ], pair_bank[:, SEQ:2 * SEQ]]
        bank += [ctx.enter_context(nc.psum_tensor(f"bank{i}", [P, SEQ], F32))[:] for i in (2, 3)]

        x_loaded = [sem(f"x_loaded{k}") for k in range(KD)]
        const_loaded = sem("const_loaded")
        w_loaded = [sem(f"w_loaded{i}") for i in range(RING)]
        whi_done = sem("whi_done")
        wlo_done = sem("wlo_done")
        unit_done = sem("unit_done")
        acc_read = [sem(f"acc_read{i}") for i in range(RING)]
        consts_made = sem("consts_made")
        sq_done = sem("sq_done")
        xg_hi_done = sem("xg_hi_done")
        xg_lo_done = sem("xg_lo_done")
        sum_done = sem("sum_done")
        gains_loaded = sem("gains_loaded")
        hbias_made = sem("hbias_made")
        sumsq_done = sem("sumsq_done")
        mean_done = sem("mean_done")
        rms_done = sem("rms_done")
        rstd_done = sem("rstd_done")
        silu_done = sem("silu_done")
        prod_done = sem("prod_done")
        hid_hi_done = sem("hid_hi_done")
        hid_lo_done = sem("hid_lo_done")
        raw_done = sem("raw_done")
        turned = sem("turned")
        rope_step = sem("rope_step")
        op_hi_done = sem("op_hi_done")
        op_lo_done = sem("op_lo_done")
        z_done = sem("z_done")
        soft_step = sem("soft_step")
        sp_step = sem("sp_step")
        sp_split = sem("sp_split")
        suffix_done = sem("suffix_done")
        a_done = sem("a_done")
        a_hi_done = sem("a_hi_done")
        a_split = sem("a_split")
        pv_done = sem("pv_done")
        ys_hi_done = sem("ys_hi_done")
        ys_done = sem("ys_done")
        ds_done = sem("ds_done")
        max_step = sem("max_step")
        p_done = sem("p_done")
        p_step = sem("p_step")
        pt_turned = sem("pt_turned")
        pt_hi_done = sem("pt_hi_done")
        pt_split = sem("pt_split")
        dpv_done = sem("dpv_done")
        yd_hi_done = sem("yd_hi_done")
        yd_done = sem("yd_done")
        gate_done = sem("gate_done")
        merge_step = sem("merge_step")
        mg_hi_done = sem("mg_hi_done")
        mg_lo_done = sem("mg_lo_done")
        y_ready = sem("y_ready")
        out_stored = sem("out_stored")
        N_CONST = 10

        def reads(u0, i):
            n = len([u for u in range(u0 % RING, u0, RING) if not MIX <= u < GATE])
            return n + i

        block = ctx.enter_context(nc.Block())

        @block.sync
        def _(sp):
            def load(u0, i, src):
                s = u0 % RING
                if u0 >= RING:
                    sp.wait_ge(wlo_done, 4 * i + (u0 - RING + 1))
                sp.dma_start(w_raw[:, s, 0:src.shape[-1]], src).then_inc(w_loaded[s], 16)

            def ffn(base, w13, w2, first):
                for c, (f0, n) in enumerate(CHUNKS):
                    u = chunk_base(base, c)
                    i0 = 0
                    if first and c == 0:
                        i0 = 1
                    if i0 == 1:
                        u += RING
                    with sp.Fori(0, n // 2 - i0) as i:
                        for j in range(4):
                            load(u + j, i, w13[4 * i + (2 * f0 + 4 * i0 + j)])
                    u += 4 * (n // 2 - i0)
                    for m in range(KD):
                        load(u + m, 0, w2[m, :, f0 * P:(f0 + n) * P])

            sp.dma_start(gains[:], A["gains"]).then_inc(gains_loaded, 16)
            for k in range(KD):
                sp.dma_start(x[:, k, :], A["xT"][:, k, :]).then_inc(x_loaded[k], 16)
                if k < RING:
                    load(k, 0, A["w13a"][k])
            for t, name in ((bias, "bias"), (cos, "cos"), (sin, "sin"), (rot, "rot"), (identf, "identf"),
                            (trif, "trif"), (identb, "identb"), (mask_sb, "mask_sb"), (mask_g0, "mask_g0"),
                            (mask_g12, "mask_g12")):
                dst = t if name == "trif" else t[:]
                if name[0:4] == "mask" or name == "identb":
                    dst = dst.bitcast(mybir.dt.uint16)
                sp.dma_start(dst, A[name]).then_inc(const_loaded, 16)
            ffn(FFN_A, A["w13a"], A["w2a"], True)
            with sp.Fori(0, (MIX_UNITS - 2) // 4) as i:
                for j in range(4):
                    load(MIX + j, i, A["wmix"][4 * i + j])
            for u in range(GATE - 2, GATE):
                load(u, 0, A["wmix"][u - MIX])
            with sp.Fori(0, KD // 4) as i:
                for j in range(4):
                    load(GATE + j, i, A["wgate"][4 * i + j])
            with sp.Fori(0, KD // 4) as i:
                for j in range(12):
                    c, n = END_COLS[j % 3]
                    load(END + j, 3 * i, A["wend"][4 * i + j // 3, :, c:c + n])
            with sp.Fori(0, KD // 4) as i:
                for j in range(4):
                    load(WO + j, i, A["wo"][4 * i + j])
            ffn(FFN_B, A["w13b"], A["w2b"], False)
            for m in range(KD):
                sp.wait_ge(y_ready, m + 1)
                sp.dma_start(out[:, m, :], x[:, m, :]).then_inc(out_stored, 16)
            sp.wait_ge(out_stored, 16 * KD)

        @block.scalar
        def _(act):
            def split_hi(u0, i, width):
                s = u0 % RING
                act.wait_ge(w_loaded[s], 16 * i + 16 * (u0 // RING + 1))
                if u0 >= RING:
                    act.wait_ge(unit_done, 4 * i + (u0 - RING + 1))
                act.activation(w_hi[:, s, 0:width], w_raw[:, s, 0:width], ACT.Copy).then_inc(whi_done, 1)

            def square(m, n):
                if m >= 3:
                    act.wait_ge(sum_done, (KD - 1) * n + m - 2)
                dst = sq[:, m % 2, :] if m else ssum[:]
                act.activation(dst, x[:, m, :], ACT.Square).then_inc(sq_done, 1)

            def rms(n):
                act.wait_ge(mean_done, n + 1)
                act.activation(mean[:], mean[:], ACT.Sqrt).then_inc(rms_done, 1)

            def up_pair(base, fbase, c, i, tail, n_norm=None):
                for j in (0, 1):
                    u = base + 2 * j
                    for v in (u + 2, u + 3):
                        split_hi(v, i, unit_width(v) if tail else KD * P)
                    if n_norm is not None and j == 0:
                        rms(n_norm)
                    act.wait_ge(acc_read[u % RING], reads(u, i) + 1)
                    act.activation(act_gate[:, j, :], gate[:, j, :], ACT.Silu).then_inc(silu_done, 1)
                    act.wait_ge(prod_done, 2 * i + (fbase + j + 1))
                    act.activation(hid_hi[:, 2 * i + (j + c), :], prod[:, j, :], ACT.Copy).then_inc(hid_hi_done, 1)

            def ffn(base, fb, n_norm, n_next):
                for c, (f0, n) in enumerate(CHUNKS):
                    u = chunk_base(base, c)
                    lastpair = 1 if c == len(CHUNKS) - 1 else 0
                    lo = 1 if c == 0 else 0
                    if lo:
                        up_pair(u, fb + f0, 0, 0, True, n_norm)
                    with act.Fori(lo, n // 2 - lastpair) as i:
                        up_pair(u, fb + f0, 0, i, False)
                    if lastpair:
                        i = n // 2 - 1
                        up_pair(u + 4 * i, fb + f0 + 2 * i, 2 * i, 0, True)
                    u += 2 * n
                    for m in range(KD):
                        if u + m + 2 < UNITS:
                            split_hi(u + m + 2, 0, unit_width(u + m + 2))
                        if c == len(CHUNKS) - 1:
                            act.wait_ge(acc_read[(u + m) % RING], reads(u + m, 0) + 1)
                            square(m, n_next)

            split_hi(0, 0, KD * P)
            for k in range(KD):
                act.wait_ge(x_loaded[k], 16)
                square(k, 0)
                if k == 3:
                    split_hi(1, 0, KD * P)
            act.preload_act_table_set("silu_and_others")
            ffn(FFN_A, 0, 0, 1)

            for kind, w in MIX_STEPS:
                if kind == "Ua":
                    split_hi(w + 2, 0, unit_width(w + 2))
                elif kind == "norm":
                    rms(w)
                    act.preload_act_table_set("natural_log_exp_and_others")
                elif kind == "gate":
                    act.wait_ge(acc_read[w % RING], reads(w, 0) + 1)
                    act.wait_ge(hbias_made, 1)
                    act.activation(gsb[:, w - GATE, :], gsb[:, w - GATE, :], ACT.Tanh, scale=0.5,
                                   bias=hbias[:, 0, w - GATE:w - GATE + 1]).then_inc(gate_done, 1)
                elif kind == "fin":
                    what, pair, g = mix_kind(w)
                    n = w - MIX
                    if what in "qk":
                        act.wait_ge(raw_done, n + 1)
                        dst = (sq_hi if what == "q" else sk_hi)[:, pair % 2, :]
                        src = raw[:, w % 2, :]
                    elif what in ("rq", "rk"):
                        act.wait_ge(rope_step, 3 * (ROPES.index(w) + 1))
                        dst = dq_hi[pair][:, g, :] if what == "rq" else dk_hi[pair][:]
                        src = roped[:]
                    else:
                        act.wait_ge(turned, TURNED.index(w) + 1)
                        if what == "v":
                            dst = sv_hi[:, pair % 2, :, :]
                            src = acc[w % RING][:].rearrange("p (b c) -> p b c", b=BLK)
                        else:
                            dst = dv_hi[pair][:]
                            src = acc[w % RING][:].rearrange("p (b c) -> p b c", b=DIL)
                    if what == "q" or what == "k":
                        if pair >= 2 and what == "q":
                            act.wait_ge(z_done, 3 * (2 * pair - 2))
                    if what == "v" and pair >= 2:
                        act.wait_ge(pv_done, 2 * pair - 2)
                    if what == "rq" and g == 0 and pair == 1:
                        act.wait_ge(pv_done, 2 * SB_PAIRS)
                    act.activation(dst, src, ACT.Copy).then_inc(op_hi_done, 1)
                elif kind == "scores":
                    for b in range(3):
                        t = 3 * w + b
                        e = ebuf[:, SB_AT[b]:SB_AT[b] + SB_WIDTH[b]]
                        act.wait_ge(z_done, t + 1)
                        if w:
                            act.wait_ge(a_split, 3 * (w - 1) + b + 1)
                        act.activation(e, bank[b][:, 0:SB_WIDTH[b]], ACT.Abs).then_inc(soft_step, 1)
                        act.wait_ge(soft_step, 3 * t + 1)
                        act.activation(e, e, ACT.Exp, scale=-1.0).then_inc(soft_step, 1)
                        act.wait_ge(soft_step, 3 * t + 2)
                        act.activation(e, e, ACT.Ln, bias=1.0).then_inc(soft_step, 1)
                elif kind == "suffix":
                    if w == 2 * SB_PAIRS - 1:
                        act.preload_act_table_set("exp_and_others")
                    for b in range(3):
                        act.wait_ge(suffix_done, 3 * w + b + 1)
                        act.activation(ebuf[:, SB_AT[b]:SB_AT[b] + SB_WIDTH[b]], bank[b][:, 0:SB_WIDTH[b]],
                                       ACT.Exp).then_inc(a_done, 1)
                elif kind == "y":
                    rows = slice(HD * (w % 2), HD * (w % 2) + HD)
                    act.wait_ge(pv_done, w + 1)
                    act.activation(ys_hi[rows, w // 2, :], bank[3][rows, :], ACT.Copy).then_inc(ys_hi_done, 1)
                elif kind == "dscores":
                    n = DIL * w[0] + w[1]
                    act.wait_ge(max_step, 2 * (n + 1))
                    if n >= 2:
                        act.wait_ge(pt_turned, n - 1)
                    if n == 0:
                        act.wait_ge(pv_done, 2 * SB_PAIRS)
                    act.activation(prob[:, n % 2, :], pair_bank[:, 0:6 * P], ACT.Exp,
                                   bias=stats[:, n % 2, 1:2], scale=HD ** -0.5,
                                   accum_out=stats[:, n % 2, 2:3]).then_inc(p_done, 1)
                elif kind == "dturn":
                    j, r = w
                    n = DIL * j + r
                    act.wait_ge(pt_turned, n + 1)
                    if r == 0 and j:
                        act.wait_ge(dpv_done, j)
                    act.activation(pT_hi[:, :, r * P:(r + 1) * P], bank[2].rearrange("p (b c) -> p b c", b=DIL),
                                   ACT.Copy).then_inc(pt_hi_done, 1)
                elif kind == "dy":
                    rows = slice(HD * (w % 2), HD * (w % 2) + HD)
                    act.wait_ge(dpv_done, w + 1)
                    act.activation(yd_hi[rows, w // 2, :].rearrange("c (p r) -> c r p", r=DIL),
                                   bank[3][rows, :].rearrange("c (r p) -> c r p", r=DIL),
                                   ACT.Copy).then_inc(yd_hi_done, 1)

            for i in range(KD // 4):
                for j in range(12):
                    v = END + 12 * i + j + 2
                    split_hi(v, 0, unit_width(v))
                    m = 4 * i + j // 3
                    if j % 3 == 0:
                        act.wait_ge(acc_read[(END + j) % RING], reads(END + j, 3 * i) + 1)
                        act.activation(gdl[:, j // 3 % 2, :], gdl[:, j // 3 % 2, :], ACT.Tanh, scale=0.5,
                                       bias=hbias[:, 1, m:m + 1]).then_inc(gate_done, 1)
                    if j % 3 == 2:
                        act.wait_ge(merge_step, m + 1)
                        act.activation(mg_hi[:, m, :], part[:, 0, :], ACT.Copy, scale=0.5).then_inc(mg_hi_done, 1)
            for m in range(KD):
                split_hi(WO + m + 2, 0, KD * P)
                act.wait_ge(acc_read[(WO + m) % RING], reads(WO + m, 0) + 1)
                square(m, 2)
            act.preload_act_table_set("silu_and_others")
            ffn(FFN_B, NF, 2, 3)
            rms(3)

        @block.vector
        def _(dve):
            def split_lo(u0, i, width):
                s = u0 % RING
                dve.wait_ge(whi_done, 4 * i + (u0 + 1))
                if u0 >= RING:
                    dve.wait_ge(unit_done, 4 * i + (u0 - RING + 1))
                dve.tensor_tensor(w_lo[:, s, 0:width], w_raw[:, s, 0:width], w_hi[:, s, 0:width].bitcast(F32),
                                  ALU.subtract).then_inc(wlo_done, 1)

            def prep(m, n):
                g = gains[:, n, m:m + 1]
                dve.tensor_scalar(xg_hi[:, m, :], x[:, m, :], g, None, ALU.mult).then_inc(xg_hi_done, 1)
                dve.wait_ge(xg_hi_done, KD * n + m + 1)
                dve.scalar_tensor_tensor(xg_lo[:, m, :], x[:, m, :], g, xg_hi[:, m, :].bitcast(F32),
                                         ALU.mult, ALU.subtract).then_inc(xg_lo_done, 1)

            def add_square(m, n):
                if m:
                    dve.wait_ge(sq_done, KD * n + m + 1)
                    if m > 1:
                        dve.wait_ge(sum_done, (KD - 1) * n + m - 1)
                    dve.tensor_tensor(ssum[:], ssum[:], sq[:, m % 2, :], ALU.add).then_inc(sum_done, 1)

            def norm(n):
                dve.wait_ge(sumsq_done, n + 1)
                dve.tensor_scalar(mean[:], bank[0], 1.0 / D, EPS, ALU.mult, ALU.add).then_inc(mean_done, 1)
                dve.wait_ge(rms_done, n + 1)
                dve.reciprocal(rstd[:], mean[:]).then_inc(rstd_done, 1)
                dve.wait_ge(rstd_done, n + 1)

            def up_pair(base, fbase, c, i, tail, n_norm=None):
                for j in (0, 1):
                    u = base + 2 * j
                    for v in (u + 2, u + 3):
                        split_lo(v, i, unit_width(v) if tail else KD * P)
                    if n_norm is not None and j == 0:
                        norm(n_norm)
                    for t, dst in ((0, gate), (1, up)):
                        s = (u + t) % RING
                        dve.wait_ge(unit_done, 4 * i + (u + t + 1))
                        dve.tensor_tensor(dst[:, j, :], acc[s][:], rstd[:], ALU.mult).then_inc(acc_read[s], 1)
                    dve.wait_ge(silu_done, 2 * i + (fbase + j + 1))
                    dve.wait_ge(acc_read[s], reads(u + 1, i) + 1)
                    dve.tensor_tensor(prod[:, j, :], act_gate[:, j, :], up[:, j, :], ALU.mult).then_inc(prod_done, 1)
                    dve.wait_ge(hid_hi_done, 2 * i + (fbase + j + 1))
                    dve.tensor_tensor(hid_lo[:, 2 * i + (j + c), :], prod[:, j, :],
                                      hid_hi[:, 2 * i + (j + c), :].bitcast(F32), ALU.subtract).then_inc(hid_lo_done, 1)

            def update_x(u, m, scale):
                s = u % RING
                dve.wait_ge(unit_done, u + 1)
                dve.scalar_tensor_tensor(x[:, m, :], acc[s][:], scale, x[:, m, :], ALU.mult,
                                         ALU.add).then_inc(acc_read[s], 1)
                return s, reads(u, 0)

            def ffn(base, fb, n_norm, n_next):
                for c, (f0, n) in enumerate(CHUNKS):
                    u = chunk_base(base, c)
                    lastpair = 1 if c == len(CHUNKS) - 1 else 0
                    lo = 1 if c == 0 else 0
                    if lo:
                        up_pair(u, fb + f0, 0, 0, True, n_norm)
                    with dve.Fori(lo, n // 2 - lastpair) as i:
                        up_pair(u, fb + f0, 0, i, False)
                    if lastpair:
                        i = n // 2 - 1
                        up_pair(u + 4 * i, fb + f0 + 2 * i, 2 * i, 0, True)
                    u += 2 * n
                    for m in range(KD):
                        if u + m + 2 < UNITS:
                            split_lo(u + m + 2, 0, unit_width(u + m + 2))
                        s, before = update_x(u + m, m, 0.5)
                        if c == len(CHUNKS) - 1:
                            if n_next < 3:
                                dve.wait_ge(acc_read[s], before + 1)
                                prep(m, n_next)
                            add_square(m, n_next)

            def take_out(w):
                what, pair, g = mix_kind(w)
                if w - 2 >= MIX:
                    dve.wait_ge(op_lo_done, w - 2 - MIX + 1)
                dve.wait_ge(unit_done, w + 1)
                if what == "q":
                    dve.scalar_tensor_tensor(raw[:, w % 2, :], acc[w % RING][:], HD ** -0.5, rstd[:], ALU.mult,
                                             ALU.mult).then_inc(raw_done, 1)
                elif what == "rv":
                    dve.tensor_tensor(raw[:, w % 2, :].rearrange("c (r p) -> c p r", r=DIL),
                                      acc[w % RING][:].rearrange("c (p r) -> c p r", r=DIL),
                                      rstd[:].rearrange("c (p r) -> c p r", r=DIL), ALU.mult).then_inc(raw_done, 1)
                else:
                    dve.tensor_tensor(raw[:, w % 2, :], acc[w % RING][:], rstd[:], ALU.mult).then_inc(raw_done, 1)

            dve.memset(ones[:], 1.0).then_inc(consts_made, 1)
            dve.wait_ge(gains_loaded, 16)
            split_lo(0, 0, KD * P)
            for k in range(KD):
                dve.wait_ge(x_loaded[k], 16)
                prep(k, 0)
                add_square(k, 0)
                if k == 3:
                    split_lo(1, 0, KD * P)
            dve.wait_ge(const_loaded, 16 * N_CONST)
            dve.tensor_scalar(hbias[:], bias[:], 0.5, None, ALU.mult).then_inc(hbias_made, 1)
            dve.memset(negones[:].bitcast(F32), -1.0).then_inc(consts_made, 1)
            dve.tensor_copy(tri[:], trif).then_inc(consts_made, 1)
            dve.wait_ge(consts_made, 3)
            ffn(FFN_A, 0, 0, 1)

            for kind, w in MIX_STEPS:
                if kind == "Ua":
                    split_lo(w + 2, 0, unit_width(w + 2))
                elif kind == "norm":
                    norm(w)
                    take_out(MIX)
                elif kind == "gate":
                    dve.wait_ge(unit_done, w + 1)
                    dve.wait_ge(dpv_done, 2)
                    dve.tensor_tensor(gsb[:, w - GATE, :], acc[w % RING][:], rstd[:],
                                      ALU.mult).then_inc(acc_read[w % RING], 1)
                elif kind == "Ub":
                    if MIX < w < GATE:
                        take_out(w)
                elif kind == "fin":
                    what, pair, g = mix_kind(w)
                    n = w - MIX
                    fin = n + 1
                    src = raw[:, w % 2, :]
                    if what in "qk":
                        hi, lo = (sq_hi, sq_lo) if what == "q" else (sk_hi, sk_lo)
                        dve.wait_ge(op_hi_done, fin)
                        dve.tensor_tensor(lo[:, pair % 2, :], src, hi[:, pair % 2, :].bitcast(F32),
                                          ALU.subtract).then_inc(op_lo_done, 1)
                    elif what in ("rq", "rk"):
                        t = 3 * ROPES.index(w)
                        if t:
                            dve.wait_ge(op_lo_done, n)
                        dve.wait_ge(raw_done, fin)
                        dve.tensor_tensor(rope1[:], src, cos[:], ALU.mult).then_inc(rope_step, 1)
                        dve.wait_ge(turned, TURNED.index(w) + 1)
                        dve.tensor_tensor(rope2[:], acc[w % RING][:], sin[:], ALU.mult).then_inc(rope_step, 1)
                        dve.wait_ge(rope_step, t + 2)
                        dve.tensor_tensor(roped[:].rearrange("c (r p) -> c p r", r=DIL),
                                          rope1[:].rearrange("c (p r) -> c p r", r=DIL),
                                          rope2[:].rearrange("c (p r) -> c p r", r=DIL),
                                          ALU.add).then_inc(rope_step, 1)
                        hi = dq_hi[pair][:, g, :] if what == "rq" else dk_hi[pair][:]
                        lo = dq_lo[pair][:, g, :] if what == "rq" else dk_lo[pair][:]
                        dve.wait_ge(rope_step, t + 3)
                        dve.wait_ge(op_hi_done, fin)
                        dve.tensor_tensor(lo, roped[:], hi.bitcast(F32), ALU.subtract).then_inc(op_lo_done, 1)
                    elif what == "v":
                        dve.wait_ge(op_hi_done, fin)
                        dve.tensor_tensor(sv_lo[:, pair % 2, :, :],
                                          acc[w % RING][:].rearrange("p (b c) -> p b c", b=BLK),
                                          sv_hi[:, pair % 2, :, :].bitcast(F32), ALU.subtract).then_inc(op_lo_done, 1)
                    else:
                        dve.wait_ge(op_hi_done, fin)
                        dve.tensor_tensor(dv_lo[pair][:], acc[w % RING][:].rearrange("p (b c) -> p b c", b=DIL),
                                          dv_hi[pair][:].bitcast(F32), ALU.subtract).then_inc(op_lo_done, 1)
                elif kind == "scores":
                    for b in range(3):
                        t = 3 * w + b
                        cols = slice(SB_AT[b], SB_AT[b] + SB_WIDTH[b])
                        dve.wait_ge(soft_step, 3 * t + 3)
                        dve.scalar_tensor_tensor(ebuf[:, cols], bank[b][:, 0:SB_WIDTH[b]], 0.0, ebuf[:, cols],
                                                 ALU.max, ALU.add).then_inc(sp_step, 1)
                        dve.wait_ge(sp_step, 2 * t + 1)
                        if w:
                            dve.wait_ge(pv_done, w)
                        dve.tensor_copy(spA_hi[:, cols], ebuf[:, cols]).then_inc(sp_step, 1)
                        dve.wait_ge(sp_step, 2 * t + 2)
                        dve.tensor_tensor(spA_lo[:, cols], ebuf[:, cols], spA_hi[:, cols].bitcast(F32),
                                          ALU.subtract).then_inc(sp_split, 1)
                elif kind == "suffix":
                    for b in range(3):
                        t = 3 * w + b
                        cols = slice(SB_AT[b], SB_AT[b] + SB_WIDTH[b])
                        dve.wait_ge(a_done, t + 1)
                        dve.wait_ge(suffix_done, 3 * w + 3)
                        dve.tensor_copy(spA_hi[:, cols], ebuf[:, cols]).then_inc(a_hi_done, 1)
                        dve.wait_ge(a_hi_done, t + 1)
                        dve.tensor_tensor(spA_lo[:, cols], ebuf[:, cols], spA_hi[:, cols].bitcast(F32),
                                          ALU.subtract).then_inc(a_split, 1)
                elif kind == "y":
                    rows = slice(HD * (w % 2), HD * (w % 2) + HD)
                    dve.wait_ge(ys_hi_done, w + 1)
                    dve.tensor_tensor(ys_lo[rows, w // 2, :], bank[3][rows, :], ys_hi[rows, w // 2, :].bitcast(F32),
                                      ALU.subtract).then_inc(ys_done, 1)
                elif kind == "dscores":
                    j, r = w
                    n = DIL * j + r
                    t = stats[:, n % 2, :]
                    dve.wait_ge(ds_done, n + 1)
                    dve.tensor_reduce(t[:, 0:1], pair_bank[:, 0:6 * P], AX.X, ALU.max).then_inc(max_step, 1)
                    dve.wait_ge(max_step, 2 * n + 1)
                    dve.tensor_scalar(t[:, 1:2], t[:, 0:1], -HD ** -0.5, None, ALU.mult).then_inc(max_step, 1)
                elif kind == "dadd":
                    j, r = w
                    n = DIL * j + r
                    t = stats[:, n % 2, :]
                    p = prob[:, n % 2, :]
                    own = p[:, r * P:(r + 1) * P]
                    dve.wait_ge(p_done, n + 1)
                    dve.reciprocal(t[:, 3:4], t[:, 2:3]).then_inc(p_step, 1)
                    dve.wait_ge(p_step, 4 * n + 1)
                    dve.tensor_scalar(p[:, 0:SEQ], p[:, 0:SEQ], t[:, 3:4], None, ALU.mult).then_inc(p_step, 1)
                    for g in (1, 2):
                        dve.wait_ge(p_step, 4 * n + 1 + g)
                        dve.scalar_tensor_tensor(own, p[:, SEQ + (g - 1) * P:SEQ + g * P], t[:, 3:4], own,
                                                 ALU.mult, ALU.add).then_inc(p_step, 1)
                elif kind == "dlo":
                    j, r = w
                    n = DIL * j + r
                    if r == 0 and j:
                        dve.wait_ge(dpv_done, j)
                    dve.wait_ge(pt_hi_done, n + 1)
                    dve.tensor_tensor(pT_lo[:, :, r * P:(r + 1) * P], bank[2].rearrange("p (b c) -> p b c", b=DIL),
                                      pT_hi[:, :, r * P:(r + 1) * P].bitcast(F32), ALU.subtract).then_inc(pt_split, 1)
                elif kind == "dy":
                    rows = slice(HD * (w % 2), HD * (w % 2) + HD)
                    dve.wait_ge(yd_hi_done, w + 1)
                    natural = lambda t: t[rows, w // 2, :].rearrange("c (p r) -> c r p", r=DIL)
                    dve.tensor_tensor(natural(yd_lo), bank[3][rows, :].rearrange("c (r p) -> c r p", r=DIL),
                                      natural(yd_hi).bitcast(F32), ALU.subtract).then_inc(yd_done, 1)

            for i in range(KD // 4):
                for j in range(12):
                    u, v = END + j, END + 12 * i + j + 2
                    s = u % RING
                    m = 4 * i + j // 3
                    split_lo(v, 0, unit_width(v))
                    dve.wait_ge(unit_done, 12 * i + (u + 1))
                    if j % 3 == 0:
                        dve.tensor_tensor(gdl[:, j // 3 % 2, :], acc[s][:], rstd[:], ALU.mult).then_inc(acc_read[s], 1)
                    elif j % 3 == 1:
                        if m:
                            dve.wait_ge(mg_lo_done, m)
                        dve.scalar_tensor_tensor(part[:, 0, :], gsb[:, m, :], 1.0, acc[s][:], ALU.add,
                                                 ALU.mult).then_inc(acc_read[s], 1)
                    else:
                        dve.wait_ge(gate_done, m + (KD + 1))
                        dve.scalar_tensor_tensor(part[:, 1, :], gdl[:, j // 3 % 2, :], 1.0, acc[s][:], ALU.add,
                                                 ALU.mult).then_inc(acc_read[s], 1)
                        dve.wait_ge(acc_read[s], reads(u, 3 * i) + 1)
                        dve.wait_ge(acc_read[(u - 1) % RING], reads(u - 1, 3 * i) + 1)
                        dve.tensor_tensor(part[:, 0, :], part[:, 0, :], part[:, 1, :], ALU.add).then_inc(merge_step, 1)
                        dve.wait_ge(merge_step, m + 1)
                        dve.wait_ge(mg_hi_done, m + 1)
                        dve.scalar_tensor_tensor(mg_lo[:, m, :], part[:, 0, :], 0.5, mg_hi[:, m, :].bitcast(F32),
                                                 ALU.mult, ALU.subtract).then_inc(mg_lo_done, 1)
            for m in range(KD):
                split_lo(WO + m + 2, 0, KD * P)
                s, before = update_x(WO + m, m, 1.0)
                dve.wait_ge(acc_read[s], before + 1)
                prep(m, 2)
                add_square(m, 2)
            ffn(FFN_B, NF, 2, 3)
            norm(3)
            for m in range(KD):
                dve.scalar_tensor_tensor(x[:, m, :], x[:, m, :], gains[:, 3, m:m + 1], rstd[:], ALU.mult,
                                         ALU.mult).then_inc(y_ready, 1)

        @block.tensor
        def _(pe):
            def product(o, w_h, w_l, r_h, r_l, first, last, check=False):
                pe.matmul(o, w_h, r_h, start=first, stop=False, skip_group_check=check)
                pe.matmul(o, w_h, r_l, start=False, stop=False, skip_group_check=check)
                return pe.matmul(o, w_l, r_h, start=False, stop=last, skip_group_check=check)

            def bank_free(u0, i):
                last = u0 - RING
                if last < 0:
                    return
                if not MIX <= last < GATE:
                    pe.wait_ge(acc_read[u0 % RING], reads(u0, i))
                    return
                kind = mix_kind(last)[0]
                if kind in ("q", "k"):
                    pe.wait_ge(raw_done, last - MIX + 1)
                elif kind in ("rq", "rk"):
                    pe.wait_ge(rope_step, 3 * ROPES.index(last) + 2)
                else:
                    pe.wait_ge(op_lo_done, last - MIX + 1)

            def unit(u0, i, rhs, ks, before=None, half=None):
                s = u0 % RING
                n = len(ks)
                lo, hi = {None: (0, n), 0: (0, n // 2), 1: (n // 2, n)}[half]
                if half != 1:
                    pe.wait_ge(wlo_done, 4 * i + (u0 + 1))
                    bank_free(u0, i)
                for k in range(lo, hi):
                    if before:
                        before(k)
                    r_h, r_l = rhs(ks[k])
                    mm = product(acc[s][:], w_hi[:, s, k * P:(k + 1) * P], w_lo[:, s, k * P:(k + 1) * P], r_h, r_l,
                                 k == 0, k == n - 1)
                if half != 0:
                    mm.then_inc(unit_done, 1)

            xg = lambda k: (xg_hi[:, k, :], xg_lo[:, k, :])
            hid = lambda k: (hid_hi[:, k, :], hid_lo[:, k, :])
            K8 = list(range(KD))

            def norm(n):
                pe.wait_ge(sum_done, (KD - 1) * (n + 1))
                pe.matmul(bank[0], ones[:], ssum[:], start=True, stop=True).then_inc(sumsq_done, 1)

            def ffn(base, fb, n_norm):
                for c, (f0, n) in enumerate(CHUNKS):
                    u = chunk_base(base, c)
                    lo = 0
                    if c == 0:
                        lo = 1
                        unit(u, 0, xg, K8, lambda k: pe.wait_ge(xg_lo_done, KD * n_norm + k + 1))
                        norm(n_norm)
                        for j in (1, 2, 3):
                            unit(u + j, 0, xg, K8)
                    with pe.Fori(lo, n // 2) as i:
                        for j in range(4):
                            unit(u + j, i, xg, K8)
                    u += 2 * n
                    ks = list(range(n))
                    for m in range(4):
                        unit(u + m, 0, hid, ks, (lambda k: pe.wait_ge(hid_lo_done, fb + f0 + k + 1)) if m == 0 else None)
                    for m in range(4, 8):
                        unit(u + m, 0, hid, ks)

            pe.wait_ge(consts_made, 1)
            ffn(FFN_A, 0, 0)

            for kind, w in MIX_STEPS:
                if kind == "Ua":
                    unit(w, 0, xg, K8, (lambda k: pe.wait_ge(xg_lo_done, KD + k + 1)) if w == MIX else None, half=0)
                elif kind == "Ub":
                    unit(w, 0, xg, K8, (lambda k: pe.wait_ge(xg_lo_done, KD + k + 1)) if w == MIX else None, half=1)
                elif kind == "norm":
                    norm(w)
                elif kind == "fin":
                    what, pair, g = mix_kind(w)
                    if what in "qk":
                        continue
                    pe.wait_ge(raw_done, w - MIX + 1)
                    if what in ("rq", "rk"):
                        pe.matmul(acc[w % RING][:], rot[:], raw[:, w % 2, :], start=True, stop=True).then_inc(turned, 1)
                    else:
                        for b in range(BLK):
                            mm = pe.transpose(acc[w % RING][:, b * P:(b + 1) * P], raw[:, w % 2, b * P:(b + 1) * P],
                                              identf[:])
                        mm.then_inc(turned, 1)
                elif kind == "scores":
                    hp, a = w // 2, w % 2
                    rows = slice(HD * a, HD * a + HD)
                    pe.wait_ge(op_lo_done, 3 * hp + 2)
                    if w == 0:
                        pe.wait_ge(mean_done, 2)
                        pe.wait_ge(consts_made, 3)
                        pe.wait_ge(const_loaded, 16 * N_CONST)
                    for b, parts in enumerate(SB_BANKS):
                        if w:
                            pe.wait_ge(a_done, 3 * (w - 1) + b + 1)
                        for n, (i, col) in enumerate(parts):
                            o = bank[b][:, col:col + SEQ - P * i]
                            ks = slice(P * i, P * i + P)
                            product(o, sk_hi[rows, hp % 2, ks], sk_lo[rows, hp % 2, ks],
                                    sq_hi[rows, hp % 2, P * i:SEQ], sq_lo[rows, hp % 2, P * i:SEQ],
                                    n == 0, False, True)
                        for i, col in parts:
                            mm = pe.matmul(bank[b][:, col:col + P], identb[:], mask_sb[:], start=False, stop=False,
                                           skip_group_check=True)
                        mm.then_inc(z_done, 1)
                elif kind == "suffix":
                    for b, parts in enumerate(SB_BANKS):
                        need = (2, 2, 3)[b]
                        pe.wait_ge(sp_split, 3 * w + need)
                        for i, col in parts:
                            for j in range(i, BLK):
                                bj, cj = sb_block(j)
                                at = slice(SB_AT[bj] + cj, SB_AT[bj] + cj + SEQ - P * j)
                                o = bank[b][:, col + P * (j - i):col + SEQ - P * i]
                                m = tri if i == j else negones
                                pe.matmul(o, m[:], spA_hi[:, at], start=False, stop=False, skip_group_check=True)
                                mm = pe.matmul(o, m[:], spA_lo[:, at], start=False, stop=True, skip_group_check=True)
                        mm.then_inc(suffix_done, 1)
                elif kind == "pv":
                    hp = w // 2
                    pe.wait_ge(op_lo_done, 3 * hp + 3)
                    pe.wait_ge(a_split, 3 * w + 3)
                    if w:
                        pe.wait_ge(ys_done, w)
                    for i in range(BLK):
                        b, col = sb_block(i)
                        at = slice(SB_AT[b] + col, SB_AT[b] + col + SEQ - P * i)
                        mm = product(bank[3][:, P * i:SEQ], sv_hi[:, hp % 2, i, :], sv_lo[:, hp % 2, i, :],
                                     spA_hi[:, at], spA_lo[:, at], i == 0, i == BLK - 1, True)
                    mm.then_inc(pv_done, 1)
                elif kind == "dscores":
                    j, r = w
                    jp, n = j // 2, DIL * j + r
                    rows = slice(HD * (j % 2), HD * (j % 2) + HD)
                    own = slice(r * P, (r + 1) * P)
                    pe.wait_ge(op_lo_done, 3 * SB_PAIRS + (NG + 2) * jp + NG + 1)
                    if n:
                        pe.wait_ge(p_done, n)
                    else:
                        pe.wait_ge(a_done, 6 * SB_PAIRS)
                    product(bank[0], dq_hi[jp][rows, 0, own], dq_lo[jp][rows, 0, own], dk_hi[jp][rows, :],
                            dk_lo[jp][rows, :], True, False, True)
                    for g in (1, 2):
                        product(bank[1][:, (g - 1) * P:g * P], dq_hi[jp][rows, g, own], dq_lo[jp][rows, g, own],
                                dk_hi[jp][rows, own], dk_lo[jp][rows, own], g == 1, False, True)
                    pe.matmul(bank[0], identb[:], mask_g0[:, r, :], start=False, stop=True, skip_group_check=True)
                    pe.matmul(bank[1][:, 0:2 * P], identb[:], mask_g12[:], start=False, stop=True,
                              skip_group_check=True).then_inc(ds_done, 1)
                elif kind == "dturn":
                    j, r = w
                    n = DIL * j + r
                    pe.wait_ge(p_step, 4 * n + 4)
                    if n:
                        pe.wait_ge(pt_split, n)
                    for b in range(DIL):
                        mm = pe.transpose(bank[2][:, b * P:(b + 1) * P], prob[:, n % 2, b * P:(b + 1) * P], identf[:])
                    mm.then_inc(pt_turned, 1)
                elif kind == "dpv":
                    jp = w // 2
                    pe.wait_ge(op_lo_done, 3 * SB_PAIRS + (NG + 2) * (jp + 1))
                    pe.wait_ge(pt_split, DIL * (w + 1))
                    if w:
                        pe.wait_ge(yd_done, w)
                    else:
                        pe.wait_ge(ys_done, 2 * SB_PAIRS)
                    for b in range(DIL):
                        mm = product(bank[3], dv_hi[jp][:, b, :], dv_lo[jp][:, b, :],
                                     pT_hi[:, b, :], pT_lo[:, b, :], b == 0, b == DIL - 1)
                    mm.then_inc(dpv_done, 1)

            ys = lambda k: (ys_hi[:, k, :], ys_lo[:, k, :])
            yd = lambda k: (yd_hi[:, k, :], yd_lo[:, k, :])
            with pe.Fori(0, KD // 4) as i:
                for j in range(0, 12, 3):
                    unit(END + j, 3 * i, xg, K8)
                    if j == 0:
                        pe.wait_ge(ys_done, 2 * SB_PAIRS)
                        pe.wait_ge(yd_done, 2 * DL_PAIRS)
                    unit(END + j + 1, 3 * i, ys, K8[0:SB_PAIRS])
                    unit(END + j + 2, 3 * i, yd, K8[0:DL_PAIRS])
            for m in range(KD):
                unit(WO + m, 0, lambda k: (mg_hi[:, k, :], mg_lo[:, k, :]), K8,
                     (lambda k: pe.wait_ge(mg_lo_done, k + 1)) if m == 0 else None)
            ffn(FFN_B, NF, 2)
            norm(3)


def constants():
    half = HD // 2
    inv = (np.float32(10000.0) ** (-np.arange(half, dtype=np.float32) / np.float32(half))).astype(np.float32)
    ang = (np.arange(SEQ, dtype=np.float32)[:, None] * inv[None, :]).astype(np.float32).T
    row = np.arange(P) % half
    d = np.arange(P)
    rot = np.zeros((P, P), np.float32)
    low = d % HD < half
    rot[d[low] + half, d[low]] = -1.0
    rot[d[~low] - half, d[~low]] = 1.0
    i = np.arange(P)
    t = DIL * i[:, None, None, None] + np.arange(DIL)[None, :, None, None]
    s = DIL * i[None, None, None, :] + np.arange(DIL)[None, None, :, None]
    ok0 = (t - s >= 0) & (t - s <= P)
    back = i[:, None] - i[None, :]
    ok12 = np.concatenate([back >= 0, (back >= 0) & (back % 4 == 0)], 1)

    def bf16_bits(v):
        return (np.asarray(v, np.float32).view(np.uint32) >> 16).astype(np.uint16)

    return {
        "cos": np.cos(ang.astype(np.float64)).astype(np.float32)[row],
        "sin": np.sin(ang.astype(np.float64)).astype(np.float32)[row],
        "rot": rot,
        "identf": np.eye(P, dtype=np.float32),
        "trif": -(i[:, None] >= i[None, :]).astype(np.float32),
        "identb": bf16_bits(np.eye(P)),
        "mask_sb": bf16_bits(np.where(i[:, None] < i[None, :], 0.0, NEG)),
        "mask_g0": bf16_bits(np.where(ok0, 0.0, NEG)).reshape(P, DIL, SEQ),
        "mask_g12": bf16_bits(np.where(ok12, 0.0, NEG)),
    }


def kernel(**inputs):
    import concourse.bacc as bacc
    from concourse.bass_utils import run_bass_kernel_spmd

    a = {k: np.asarray(v) for k, v in inputs.items()}

    def units(w):
        k, m = w.shape
        return w.reshape(k // P, P, m // P, P).transpose(2, 1, 0, 3).reshape(m // P, P, k)

    def pairs(w1, w3):
        return np.stack([units(w1), units(w3)], 1).reshape(2 * NF, P, D)

    win = units(a["w_in"][0])
    SBT, DQT = SB_PAIRS, NG * DL_PAIRS
    order = []
    for hp in range(SB_PAIRS):
        order += [hp, SBT + hp, 2 * SBT + hp]
    dq, dk = 3 * SBT, 3 * SBT + DQT
    for jp in range(DL_PAIRS):
        order += [dq + DL_PAIRS * g + jp for g in range(NG)] + [dk + jp, dk + DL_PAIRS + jp]
    gate0 = dk + 2 * DL_PAIRS
    wend = np.concatenate([win[gate0 + KD:gate0 + 2 * KD], units(a["w_sb_out"][0]),
                           units(a["w_dil_out"][0])], 2)
    cols = lambda v: v.reshape(-1, P).T
    arrays = {
        "xT": a["x"][0].T.reshape(KD, P, SEQ).transpose(1, 0, 2),
        "gains": np.stack([cols(a[n].reshape(-1)) for n in ("g_ffn1", "g_mix", "g_ffn2", "g_final")], 1),
        "bias": cols(a["b_gate"][0]).reshape(P, 2, KD),
        "w13a": pairs(a["w1_a"][0], a["w3_a"][0]), "w2a": units(a["w2_a"][0]),
        "w13b": pairs(a["w1_b"][0], a["w3_b"][0]), "w2b": units(a["w2_b"][0]),
        "wmix": win[order], "wgate": win[gate0:gate0 + KD], "wend": wend, "wo": units(a["w_o"][0]),
    }
    arrays.update(constants())
    arrays = {k: np.ascontiguousarray(v) for k, v in arrays.items()}

    nc = bacc.Bacc("TRN2", target_bir_lowering=False, num_devices=1)
    A = {n: nc.dram_tensor("in_" + n, v.shape, mybir.dt.from_np(v.dtype), kind="ExternalInput").ap()
         for n, v in arrays.items()}
    out = nc.dram_tensor("out", (P, KD, SEQ), mybir.dt.float32, kind="ExternalOutput").ap()
    build(nc, A, out)
    r = run_bass_kernel_spmd(nc, [{"in_" + n: v for n, v in arrays.items()}], core_ids=[0])
    y = r.results[0]["out"]
    return np.ascontiguousarray(y.transpose(1, 0, 2).reshape(1, D, SEQ).transpose(0, 2, 1))
```

```python
from contextlib import ExitStack

import numpy as np

import concourse.bass as bass
from concourse import mybir

P = 128
SEQ = 512
D = 1024
KD = D // P
FF = 2816
NF = FF // P
CHUNKS = ((0, 8), (8, 8), (16, 6))
HD = 64
SB_PAIRS = 4
DL_PAIRS = 2
NG = 3
DIL = 4
BLK = SEQ // P
EPS = 1e-6
NEG = -1e30
RING = 4

MIX_ORDER = ([("q", 0, 0), ("k", 0, 0), ("v", 0, 0), ("q", 1, 0), ("k", 1, 0), ("v", 1, 0),
              ("rk", 0, 0), ("q", 2, 0), ("k", 2, 0), ("v", 2, 0), ("rq", 0, 0), ("rq", 0, 1),
              ("q", 3, 0), ("k", 3, 0), ("rq", 0, 2), ("v", 3, 0), ("rv", 0, 0)]
             + [("rk", 1, 0)] + [("rq", 1, g) for g in range(NG)] + [("rv", 1, 0)])
FFN_A = 0
MIX = 2 * NF + len(CHUNKS) * KD
MIX_UNITS = len(MIX_ORDER)
GATE = MIX + MIX_UNITS
END = GATE + KD
WO = END + 3 * KD
FFN_B = WO + KD
UNITS = FFN_B + 2 * NF + len(CHUNKS) * KD
POOL_LO = (MIX + 4, END)
SB_FILL = ((3, 1), (1, 1), (4, 1), (2, 2), (4, 1), (3, 1), (2, 2), (1, 1))
DL_FILL = (1, 1, 1, 1, 1, 1, 2, 3, 1, 1, 1, 2, 1, 2, 2, 2)
START_STEPS = ([("x", 0)] + [("w", (u, 0)) for u in range(RING)] + [("x", k) for k in range(1, KD // 2)]
               + [("w", (0, 1)), ("sq", 0), ("sq", 1)] + [("x", k) for k in range(KD // 2, KD)]
               + [("sq", 2), ("w", (1, 1)), ("sq", 3), ("sq", 4), ("w", (2, 1)), ("sq", 5), ("sq", 6),
                  ("w", (3, 1)), ("sq", 7)])
END_COLS = ((0, 1024), (1024, 512), (1536, 256))
SB_BANKS = (((1, 0), (3, 384)), ((2, 0),), ((0, 0),))
SB_WIDTH = (512, 256, 512)
SB_AT = (0, 512, 768)


def chunk_base(base, c):
    return base + sum(2 * n + KD for _, n in CHUNKS[:c])


def unit_width(u):
    for base in (FFN_A, FFN_B):
        for c, (_, n) in enumerate(CHUNKS):
            at = chunk_base(base, c) + 2 * n
            if at <= u < at + KD:
                return n * P
    if END <= u < WO:
        return END_COLS[(u - END) % 3][1]
    return KD * P


def sb_block(i):
    for b, parts in enumerate(SB_BANKS):
        for blk, col in parts:
            if blk == i:
                return b, col


def mix_schedule():
    s = []
    held = []
    halves = [(half, u) for u in range(MIX, END) for half in ("Ua", "Ub")]

    def fill(n):
        for _ in range(n):
            half, u = halves.pop(0)
            s.append((half, u))
            if MIX < u <= GATE and half == ("Ub" if MIX_ORDER[u - 1 - MIX][0] in ("rq", "rk") else "Ua"):
                s.append(("fin", u - 1))
            if half == "Ub" and u >= GATE:
                held.append(u)
        if ("dpv", 1) in s:
            while held:
                s.append(("gate", held.pop(0)))

    fill(2)
    s.append(("norm", 1))
    fill(4)
    s.append(("scores", 0))
    for h in range(2 * SB_PAIRS):
        fill(SB_FILL[h][0])
        if h:
            s.append(("y", h - 1))
        s.append(("suffix", h))
        if h:
            s.append(("ysplit", h - 1))
        fill(SB_FILL[h][1])
        s.append(("scores", h + 1) if h + 1 < 2 * SB_PAIRS else ("dscores", (0, 0)))
        s.append(("pv", h))
    blocks = [(j, r) for j in range(2 * DL_PAIRS) for r in range(DIL)]
    for n, (j, r) in enumerate(blocks):
        fill(DL_FILL[n] - 1)
        if n == 0:
            s.append(("y", 2 * SB_PAIRS - 1))
        if n == 1:
            s.append(("ysplit", 2 * SB_PAIRS - 1))
        if n + 1 < len(blocks):
            s.append(("dscores", blocks[n + 1]))
        s.append(("dadd", (j, r)))
        fill(1)
        if r == 0 and j:
            s.append(("dpv", j - 1))
        s.append(("dturn", (j, r)))
        s.append(("dlo", (j, r)))
        if r == 0 and j:
            s.append(("dy", j - 1))
        if r == 1 and j:
            s.append(("dysplit", j - 1))
    fill(len(halves))
    s.append(("dpv", 2 * DL_PAIRS - 1))
    s.append(("dy", 2 * DL_PAIRS - 1))
    s.append(("dysplit", 2 * DL_PAIRS - 1))
    return s


MIX_STEPS = mix_schedule()
FINS = [w for kind, w in MIX_STEPS if kind == "fin"]


def mix_kind(u):
    return MIX_ORDER[u - MIX]


def through(*units):
    return max(MIX_ORDER.index(u) for u in units) + 1


ROPES = [u for u in FINS if mix_kind(u)[0] in ("rq", "rk")]


def ropes_before(u):
    return len([w for w in ROPES if w < u])


TURNED = [u for u in FINS if mix_kind(u)[0] in ("v", "rv")]


def build(nc, A, out):
    F32, F32R, BF16 = mybir.dt.float32, mybir.dt.float32r, mybir.dt.bfloat16
    ALU, ACT, AX = mybir.AluOpType, mybir.ActivationFunctionType, mybir.AxisListType
    ctx = ExitStack()
    with ctx:
        def sb(name, shape, dt=F32, where=ctx):
            return where.enter_context(nc.sbuf_tensor(name, shape, dt))

        def sem(name):
            return ctx.enter_context(nc.semaphore(name))

        x = sb("x", [P, KD, SEQ])
        xg_hi = sb("xg_hi", [P, KD, SEQ], F32R)
        xg_lo = sb("xg_lo", [P, KD, SEQ], F32R)
        w_raw = sb("w_raw", [P, RING, KD * P])
        w_hi = sb("w_hi", [P, RING, KD * P], F32R)
        w_lo = sb("w_lo", [P, RING, KD * P], F32R)
        rstd = sb("rstd", [P, SEQ])
        gains = sb("gains", [P, 4, KD])
        bias = sb("bias", [P, 2, KD])
        hbias = sb("hbias", [P, 2, KD])
        ones = sb("ones", [P, P])
        cos = sb("cos", [P, SEQ])
        sin = sb("sin", [P, SEQ])
        identf = sb("identf", [P, P])
        tri = sb("tri", [P, P], F32R)
        negones = sb("negones", [P, P], F32R)
        identb = sb("identb", [P, P], BF16)
        mask_sb = sb("mask_sb", [P, P], BF16)
        mask_g0 = sb("mask_g0", [P, DIL, SEQ], BF16)
        mask_g12 = sb("mask_g12", [P, 2 * P], BF16)
        rope1 = sb("rope1", [P, SEQ])
        rope2 = sb("rope2", [P, SEQ])
        roped = sb("roped", [P, SEQ])
        ysum = sb("ysum", [P, SEQ])
        stats = sb("stats", [P, 2, 4])
        col = sb("col", [P, BLK])
        mean = rope1
        diag = rope2

        with ExitStack() as ffn:
            ssum = sb("ssum", [P, SEQ], F32, ffn)
            sq = sb("sq", [P, 2, SEQ], F32, ffn)
            hid_hi = sb("hid_hi", [P, 8, SEQ], F32R, ffn)
            hid_lo = sb("hid_lo", [P, 8, SEQ], F32R, ffn)
            gate = sb("gate", [P, 2, SEQ], F32, ffn)
            act_gate = sb("act_gate", [P, 2, SEQ], F32, ffn)
            up = sb("up", [P, 2, SEQ], F32, ffn)
            prod = sb("prod", [P, 2, SEQ], F32, ffn)
            trif = prod[:, 1, 0:P]
        with ExitStack() as mix:
            ys_hi = sb("ys_hi", [P, SB_PAIRS, SEQ], F32R, mix)
            ys_lo = sb("ys_lo", [P, SB_PAIRS, SEQ], F32R, mix)
            yd_hi = sb("yd_hi", [P, DL_PAIRS, SEQ], F32R, mix)
            yd_lo = sb("yd_lo", [P, DL_PAIRS, SEQ], F32R, mix)
            with ExitStack() as att:
                raw = sb("raw", [P, 2, SEQ], F32, att)
                with ExitStack() as s:
                    spA_hi = sb("spA_hi", [P, 1280], F32R, s)
                    spA_lo = sb("spA_lo", [P, 1280], F32R, s)
                    ebuf = sb("ebuf", [P, 1280], F32, s)
                    sv = sb("sv", [P, 2, BLK, 2 * P], F32R, s)
                    sq_hi = sb("sq_hi", [P, 2, SEQ], F32R, s)
                    sq_lo = sb("sq_lo", [P, 2, SEQ], F32R, s)
                    sk_hi = sb("sk_hi", [P, 2, SEQ], F32R, s)
                    sk_lo = sb("sk_lo", [P, 2, SEQ], F32R, s)
                pT_hi = sb("pT_hi", [P, DIL, SEQ], F32R, att)
                pT_lo = sb("pT_lo", [P, DIL, SEQ], F32R, att)
                prob = sb("prob", [P, 2, 6 * P], F32, att)
                dq_hi = [None, None]
                dq_lo, dk_hi, dk_lo, dv = ([None, None] for _ in range(4))

                def dl_buffers(jp, where):
                    dq_hi[jp] = sb(f"dq_hi{jp}", [P, NG, SEQ], F32R, where)
                    dq_lo[jp] = sb(f"dq_lo{jp}", [P, NG, SEQ], F32R, where)
                    dk_hi[jp] = sb(f"dk_hi{jp}", [P, SEQ], F32R, where)
                    dk_lo[jp] = sb(f"dk_lo{jp}", [P, SEQ], F32R, where)
                    dv[jp] = sb(f"dv{jp}", [P, DIL, 2 * P], F32R, where)
                dl_buffers(1, att)
                with ExitStack() as s:
                    dl_buffers(0, s)
                gsb = sb("gsb", [P, KD, SEQ], F32, att)
            with ExitStack() as end:
                mg_hi = sb("mg_hi", [P, KD, SEQ], F32R, end)
                mg_lo = sb("mg_lo", [P, KD, SEQ], F32R, end)
                gdl = sb("gdl", [P, 2, SEQ], F32, end)
                part = sb("part", [P, 2, SEQ], F32, end)

        acc = [ctx.enter_context(nc.psum_tensor(f"acc{i}", [P, SEQ], F32)) for i in range(RING)]
        pair_bank = ctx.enter_context(nc.psum_tensor("pair_bank", [P, 2 * SEQ], F32))
        bank = [pair_bank[:, 0:SEQ], pair_bank[:, SEQ:2 * SEQ]]
        bank += [ctx.enter_context(nc.psum_tensor(f"bank{i}", [P, SEQ], F32))[:] for i in (2, 3)]

        x_loaded = [sem(f"x_loaded{k}") for k in range(KD)]
        const_loaded = sem("const_loaded")
        w_loaded = [sem(f"w_loaded{i}") for i in range(RING)]
        half_loaded = [sem(f"half_loaded{i}") for i in range(RING)]
        half_hi_done = sem("half_hi_done")
        half_lo_done = sem("half_lo_done")
        whi_done = sem("whi_done")
        wlo_done = sem("wlo_done")
        pool_lo_done = sem("pool_lo_done")
        unit_done = sem("unit_done")
        acc_read = [sem(f"acc_read{i}") for i in range(RING)]
        consts_made = sem("consts_made")
        sq_done = sem("sq_done")
        xg_hi_done = sem("xg_hi_done")
        xg_lo_done = sem("xg_lo_done")
        sum_done = sem("sum_done")
        gains_loaded = sem("gains_loaded")
        hbias_made = sem("hbias_made")
        sumsq_done = sem("sumsq_done")
        mean_done = sem("mean_done")
        rms_done = sem("rms_done")
        rstd_done = sem("rstd_done")
        diag_done = sem("diag_done")
        spread_done = sem("spread_done")
        silu_done = sem("silu_done")
        prod_done = sem("prod_done")
        hid_hi_done = sem("hid_hi_done")
        hid_lo_done = sem("hid_lo_done")
        raw_done = sem("raw_done")
        turned = sem("turned")
        rotated = sem("rotated")
        rope_step = sem("rope_step")
        op_hi_done = sem("op_hi_done")
        op_lo_done = sem("op_lo_done")
        z_done = sem("z_done")
        soft_step = sem("soft_step")
        sp_step = sem("sp_step")
        sp_split = sem("sp_split")
        suffix_done = sem("suffix_done")
        a_done = sem("a_done")
        a_hi_done = sem("a_hi_done")
        a_split = sem("a_split")
        pv_done = sem("pv_done")
        y_cross_done = sem("y_cross_done")
        y_whole = sem("y_whole")
        ys_hi_done = sem("ys_hi_done")
        ys_done = sem("ys_done")
        ds_done = sem("ds_done")
        max_step = sem("max_step")
        p_done = sem("p_done")
        p_step = sem("p_step")
        pt_turned = sem("pt_turned")
        pt_hi_done = sem("pt_hi_done")
        pt_split = sem("pt_split")
        gate_done = sem("gate_done")
        merge_step = sem("merge_step")
        mg_hi_done = sem("mg_hi_done")
        mg_lo_done = sem("mg_lo_done")
        y_ready = sem("y_ready")
        out_stored = sem("out_stored")
        N_CONST = 9

        def wait_lo(engine, u0, i):
            first, end = POOL_LO
            if first <= u0 < end:
                engine.wait_ge(pool_lo_done, 4 * i + (u0 - first + 1))
            else:
                engine.wait_ge(wlo_done, 4 * i + (u0 + 1 if u0 < first else u0 + 1 - (end - first)))

        def head_rows(h):
            return slice(HD * (h % 2), HD * (h % 2) + HD)

        def v_parts(t):
            v = t.rearrange("p b (x c) -> p b x c", c=HD)
            return v[:, :, 0:4:2, :], v[:, :, 1:4:2, :]

        def half_cols(half):
            return slice(half * KD * P // 2, (half + 1) * KD * P // 2)

        def reads(u0, i):
            n = len([u for u in range(u0 % RING, u0, RING) if not MIX <= u < GATE])
            return n + i

        block = ctx.enter_context(nc.Block())

        @block.sync
        def _(sp):
            def load(u0, i, src):
                s = u0 % RING
                if u0 >= RING:
                    wait_lo(sp, u0 - RING, i)
                sp.dma_start(w_raw[:, s, 0:src.shape[-1]], src).then_inc(w_loaded[s], 16)

            def ffn(base, w13, w2, first):
                for c, (f0, n) in enumerate(CHUNKS):
                    u = chunk_base(base, c)
                    i0 = 0
                    if first and c == 0:
                        i0 = 1
                    if i0 == 1:
                        u += RING
                    with sp.Fori(0, n // 2 - i0) as i:
                        for j in range(4):
                            load(u + j, i, w13[4 * i + (2 * f0 + 4 * i0 + j)])
                    u += 4 * (n // 2 - i0)
                    for m in range(KD):
                        load(u + m, 0, w2[m, :, f0 * P:(f0 + n) * P])

            sp.dma_start(gains[:], A["gains"]).then_inc(gains_loaded, 16)
            for kind, w in START_STEPS:
                if kind == "x":
                    sp.dma_start(x[:, w, :], A["xT"][:, w, :]).then_inc(x_loaded[w], 16)
                elif kind == "w":
                    (u, half) = w
                    sp.dma_start(w_raw[:, u, half_cols(half)], A["w13a"][u, :, half_cols(half)]).then_inc(
                        (w_loaded if half else half_loaded)[u], 16)
            for t, name in ((bias, "bias"), (cos, "cos"), (sin, "sin"), (identf, "identf"),
                            (trif, "trif"), (identb, "identb"), (mask_sb, "mask_sb"), (mask_g0, "mask_g0"),
                            (mask_g12, "mask_g12")):
                dst = t if name == "trif" else t[:]
                if name[0:4] == "mask" or name == "identb":
                    dst = dst.bitcast(mybir.dt.uint16)
                sp.dma_start(dst, A[name]).then_inc(const_loaded, 16)
            ffn(FFN_A, A["w13a"], A["w2a"], True)
            for u in range(MIX, GATE):
                load(u, 0, A["wmix"][u - MIX])
            for u in range(GATE, END):
                load(u, 0, A["wgate"][u - GATE])
            for u in range(END, WO):
                c, n = END_COLS[(u - END) % 3]
                load(u, 0, A["wend"][(u - END) // 3, :, c:c + n])
            with sp.Fori(0, KD // 4) as i:
                for j in range(4):
                    load(WO + j, i, A["wo"][4 * i + j])
            ffn(FFN_B, A["w13b"], A["w2b"], False)
            for m in range(KD):
                sp.wait_ge(y_ready, m + 1)
                sp.dma_start(out[:, m, :], x[:, m, :]).then_inc(out_stored, 16)
            sp.wait_ge(out_stored, 16 * KD)

        @block.scalar
        def _(act):
            def split_hi(u0, i, width):
                s = u0 % RING
                act.wait_ge(w_loaded[s], 16 * i + 16 * (u0 // RING + 1))
                act.wait_ge(unit_done, 4 * i + (u0 - RING + 1))
                act.activation(w_hi[:, s, 0:width], w_raw[:, s, 0:width], ACT.Copy).then_inc(whi_done, 1)

            def square(m, n):
                if m >= 3:
                    act.wait_ge(sum_done, (KD - 1) * n + m - 2)
                dst = sq[:, m % 2, :] if m else ssum[:]
                act.activation(dst, x[:, m, :], ACT.Square).then_inc(sq_done, 1)

            def rms(n):
                act.wait_ge(mean_done, n + 1)
                act.activation(mean[:], mean[:], ACT.Sqrt).then_inc(rms_done, 1)

            def up_pair(base, fbase, slot, i, tail, n_norm=None):
                for j in (0, 1):
                    u = base + 2 * j
                    ahead = (u + 2, u + 3)
                    if n_norm == 0:
                        ahead = (RING + j,)
                    for v in ahead:
                        split_hi(v, i, unit_width(v) if tail else KD * P)
                    if n_norm is not None and j == 0:
                        rms(n_norm)
                        act.preload_act_table_set("silu_and_others")
                    act.wait_ge(acc_read[u % RING], reads(u, i) + 1)
                    act.activation(act_gate[:, j, :], gate[:, j, :], ACT.Silu).then_inc(silu_done, 1)
                    act.wait_ge(prod_done, 2 * i + (fbase + j + 1))
                    act.activation(hid_hi[:, 2 * i + (j + slot), :], prod[:, j, :], ACT.Copy).then_inc(hid_hi_done, 1)

            def ffn(base, fb, n_norm, n_next):
                for c, (f0, n) in enumerate(CHUNKS):
                    u = chunk_base(base, c)
                    lastpair = 1 if c == len(CHUNKS) - 1 else 0
                    lo = 1 if c == 0 else 0
                    if lo:
                        up_pair(u, fb + f0, 0, 0, True, n_norm)
                    with act.Fori(lo, n // 2 - lastpair) as i:
                        up_pair(u, fb + f0, 0, i, False)
                    if lastpair:
                        i = n // 2 - 1
                        up_pair(u + 4 * i, fb + f0 + 2 * i, 2 * i, 0, True)
                    u += 2 * n
                    for m in range(KD):
                        if u + m + 2 < UNITS:
                            split_hi(u + m + 2, 0, unit_width(u + m + 2))
                        if c == len(CHUNKS) - 1:
                            if m == 0:
                                act.preload_act_table_set("sqrt_and_others")
                            act.wait_ge(acc_read[(u + m) % RING], reads(u + m, 0) + 1)
                            square(m, n_next)

            act.preload_act_table_set("sqrt_and_others")
            act.wait_ge(gains_loaded, 16)
            for kind, w in START_STEPS:
                if kind == "x":
                    act.wait_ge(x_loaded[w], 16)
                    act.activation(xg_hi[:, w, :], x[:, w, :], ACT.Copy,
                                   scale=gains[:, 0, w:w + 1]).then_inc(xg_hi_done, 1)
                elif kind == "sq":
                    square(w, 0)
                else:
                    (u, half) = w
                    act.wait_ge((w_loaded if half else half_loaded)[u], 16)
                    act.activation(w_hi[:, u, half_cols(half)], w_raw[:, u, half_cols(half)],
                                   ACT.Copy).then_inc(whi_done if half else half_hi_done, 1)
            ffn(FFN_A, 0, 0, 1)

            for kind, w in MIX_STEPS:
                if kind == "Ua":
                    split_hi(w + 2, 0, unit_width(w + 2))
                elif kind == "norm":
                    rms(w)
                    act.preload_act_table_set("natural_log_exp_and_others")
                elif kind == "gate":
                    act.wait_ge(acc_read[w % RING], reads(w, 0) + 1)
                    act.wait_ge(hbias_made, 1)
                    act.activation(gsb[:, w - GATE, :], gsb[:, w - GATE, :], ACT.Tanh, scale=0.5,
                                   bias=hbias[:, 0, w - GATE:w - GATE + 1]).then_inc(gate_done, 1)
                elif kind == "fin":
                    what, pair, g = mix_kind(w)
                    n = w - MIX
                    if what in "qk":
                        act.wait_ge(raw_done, n + 1)
                        dst = (sq_hi if what == "q" else sk_hi)[:, pair % 2, :]
                        src = raw[:, w % 2, :]
                    elif what in ("rq", "rk"):
                        act.wait_ge(rope_step, 2 * (ROPES.index(w) + 1))
                        dst = dq_hi[pair][:, g, :] if what == "rq" else dk_hi[pair][:]
                        src = roped[:]
                    else:
                        act.wait_ge(turned, TURNED.index(w) + 1)
                        dst = v_parts(sv[:, pair % 2, :, :] if what == "v" else dv[pair][:])[0]
                        src = acc[w % RING][:].rearrange("p (b a c) -> p b a c", b=BLK, a=2)
                    if what == "q" or what == "k":
                        if pair >= 2 and what == "q":
                            act.wait_ge(z_done, 3 * (2 * pair - 2))
                    if what == "v" and pair >= 2:
                        act.wait_ge(pv_done, 2 * pair - 2)
                    if n == through(("rv", 0, 0)):
                        act.wait_ge(pv_done, 2 * SB_PAIRS)
                    act.activation(dst, src, ACT.Copy).then_inc(op_hi_done, 1)
                elif kind == "scores":
                    for b in range(3):
                        t = 3 * w + b
                        e = ebuf[:, SB_AT[b]:SB_AT[b] + SB_WIDTH[b]]
                        act.wait_ge(z_done, t + 1)
                        if w:
                            act.wait_ge(a_split, 3 * (w - 1) + b + 1)
                        act.activation(e, bank[b][:, 0:SB_WIDTH[b]], ACT.Abs).then_inc(soft_step, 1)
                        act.wait_ge(soft_step, 3 * t + 1)
                        act.activation(e, e, ACT.Exp, scale=-1.0).then_inc(soft_step, 1)
                        act.wait_ge(soft_step, 3 * t + 2)
                        act.activation(e, e, ACT.Ln, bias=1.0).then_inc(soft_step, 1)
                elif kind == "suffix":
                    if w == 2 * SB_PAIRS - 1:
                        act.preload_act_table_set("exp_and_others")
                    for b in range(3):
                        act.wait_ge(suffix_done, 3 * w + b + 1)
                        act.activation(ebuf[:, SB_AT[b]:SB_AT[b] + SB_WIDTH[b]], bank[b][:, 0:SB_WIDTH[b]],
                                       ACT.Exp).then_inc(a_done, 1)
                elif kind in ("y", "dy"):
                    rows, other = head_rows(w), head_rows(w + 1)
                    n = w + (2 * SB_PAIRS if kind == "dy" else 0)
                    act.wait_ge(pv_done, n + 1)
                    if n >= 2:
                        act.wait_ge(ys_done, n - 1)
                    act.activation(ysum[rows, :], bank[3][other, :], ACT.Copy).then_inc(y_cross_done, 1)
                elif kind in ("ysplit", "dysplit"):
                    rows = head_rows(w)
                    if kind == "ysplit":
                        act.wait_ge(y_whole, w + 1)
                        act.activation(ys_hi[rows, w // 2, :], ysum[rows, :], ACT.Copy).then_inc(ys_hi_done, 1)
                    else:
                        act.wait_ge(y_whole, 2 * SB_PAIRS + w + 1)
                        act.activation(yd_hi[rows, w // 2, :].rearrange("c (p r) -> c r p", r=DIL),
                                       ysum[rows, :].rearrange("c (r p) -> c r p", r=DIL),
                                       ACT.Copy).then_inc(ys_hi_done, 1)
                elif kind == "dscores":
                    n = DIL * w[0] + w[1]
                    act.wait_ge(max_step, 2 * (n + 1))
                    if n >= 2:
                        act.wait_ge(pt_turned, n - 1)
                    if n == 0:
                        act.wait_ge(pv_done, 2 * SB_PAIRS)
                    act.activation(prob[:, n % 2, :], pair_bank[:, 0:6 * P], ACT.Exp,
                                   bias=stats[:, n % 2, 1:2], scale=HD ** -0.5,
                                   accum_out=stats[:, n % 2, 2:3]).then_inc(p_done, 1)
                elif kind == "dturn":
                    j, r = w
                    n = DIL * j + r
                    act.wait_ge(pt_turned, n + 1)
                    if r == 0 and j:
                        act.wait_ge(pv_done, 2 * SB_PAIRS + j)
                    act.activation(pT_hi[:, :, r * P:(r + 1) * P], bank[2].rearrange("p (b c) -> p b c", b=DIL),
                                   ACT.Copy).then_inc(pt_hi_done, 1)

            for i in range(KD // 4):
                for j in range(12):
                    v = END + 12 * i + j + 2
                    split_hi(v, 0, unit_width(v))
                    m = 4 * i + j // 3
                    if j % 3 == 0:
                        act.wait_ge(acc_read[(END + j) % RING], reads(END + j, 3 * i) + 1)
                        act.activation(gdl[:, j // 3 % 2, :], gdl[:, j // 3 % 2, :], ACT.Tanh, scale=0.5,
                                       bias=hbias[:, 1, m:m + 1]).then_inc(gate_done, 1)
                    if j % 3 == 2:
                        act.wait_ge(merge_step, m + 1)
                        act.activation(mg_hi[:, m, :], part[:, 0, :], ACT.Copy, scale=0.5).then_inc(mg_hi_done, 1)
            for m in range(KD):
                split_hi(WO + m + 2, 0, KD * P)
                if m == 0:
                    act.preload_act_table_set("sqrt_and_others")
                act.wait_ge(acc_read[(WO + m) % RING], reads(WO + m, 0) + 1)
                square(m, 2)
            ffn(FFN_B, NF, 2, 3)
            act.wait_ge(mean_done, 4)
            act.activation(col[:], col[:], ACT.Sqrt).then_inc(rms_done, 1)

        @block.vector
        def _(dve):
            def split_lo(u0, i, width):
                s = u0 % RING
                dve.wait_ge(whi_done, 4 * i + (u0 + 1))
                dve.wait_ge(unit_done, 4 * i + (u0 - RING + 1))
                dve.tensor_tensor(w_lo[:, s, 0:width], w_raw[:, s, 0:width], w_hi[:, s, 0:width].bitcast(F32),
                                  ALU.subtract).then_inc(wlo_done, 1)

            def prep(m, n):
                g = gains[:, n, m:m + 1]
                if n:
                    dve.tensor_scalar(xg_hi[:, m, :], x[:, m, :], g, None, ALU.mult).then_inc(xg_hi_done, 1)
                dve.wait_ge(xg_hi_done, KD * n + m + 1)
                dve.scalar_tensor_tensor(xg_lo[:, m, :], x[:, m, :], g, xg_hi[:, m, :].bitcast(F32),
                                         ALU.mult, ALU.subtract).then_inc(xg_lo_done, 1)

            def add_square(m, n):
                if m:
                    dve.wait_ge(sq_done, KD * n + m + 1)
                    if m > 1:
                        dve.wait_ge(sum_done, (KD - 1) * n + m - 1)
                    dve.tensor_tensor(ssum[:], ssum[:], sq[:, m % 2, :], ALU.add).then_inc(sum_done, 1)

            def norm(n):
                dve.wait_ge(sumsq_done, n + 1)
                dve.tensor_scalar(mean[:], bank[0], 1.0 / D, EPS, ALU.mult, ALU.add).then_inc(mean_done, 1)
                dve.wait_ge(rms_done, n + 1)
                dve.reciprocal(rstd[:], mean[:]).then_inc(rstd_done, 1)
                dve.wait_ge(rstd_done, n + 1)

            def up_pair(base, fbase, slot, i, tail, n_norm=None):
                for j in (0, 1):
                    u = base + 2 * j
                    ahead = (u + 2, u + 3)
                    if n_norm == 0:
                        ahead = (RING + j,)
                    for v in ahead:
                        split_lo(v, i, unit_width(v) if tail else KD * P)
                    if n_norm is not None and j == 0:
                        norm(n_norm)
                    for t, dst in ((0, gate), (1, up)):
                        s = (u + t) % RING
                        dve.wait_ge(unit_done, 4 * i + (u + t + 1))
                        dve.tensor_tensor(dst[:, j, :], acc[s][:], rstd[:], ALU.mult).then_inc(acc_read[s], 1)
                    dve.wait_ge(silu_done, 2 * i + (fbase + j + 1))
                    dve.wait_ge(acc_read[s], reads(u + 1, i) + 1)
                    dve.tensor_tensor(prod[:, j, :], act_gate[:, j, :], up[:, j, :], ALU.mult).then_inc(prod_done, 1)
                    dve.wait_ge(hid_hi_done, 2 * i + (fbase + j + 1))
                    dve.tensor_tensor(hid_lo[:, 2 * i + (j + slot), :], prod[:, j, :],
                                      hid_hi[:, 2 * i + (j + slot), :].bitcast(F32), ALU.subtract).then_inc(hid_lo_done, 1)

            def update_x(u, m, scale):
                s = u % RING
                dve.wait_ge(unit_done, u + 1)
                dve.scalar_tensor_tensor(x[:, m, :], acc[s][:], scale, x[:, m, :], ALU.mult,
                                         ALU.add).then_inc(acc_read[s], 1)
                return s, reads(u, 0)

            def ffn(base, fb, n_norm, n_next):
                for c, (f0, n) in enumerate(CHUNKS):
                    u = chunk_base(base, c)
                    lastpair = 1 if c == len(CHUNKS) - 1 else 0
                    lo = 1 if c == 0 else 0
                    if lo:
                        up_pair(u, fb + f0, 0, 0, True, n_norm)
                    with dve.Fori(lo, n // 2 - lastpair) as i:
                        up_pair(u, fb + f0, 0, i, False)
                    if lastpair:
                        i = n // 2 - 1
                        up_pair(u + 4 * i, fb + f0 + 2 * i, 2 * i, 0, True)
                    u += 2 * n
                    for m in range(KD):
                        if u + m + 2 < UNITS:
                            split_lo(u + m + 2, 0, unit_width(u + m + 2))
                        s, before = update_x(u + m, m, 0.5)
                        if c == len(CHUNKS) - 1:
                            if n_next < 3:
                                dve.wait_ge(acc_read[s], before + 1)
                                prep(m, n_next)
                            if n_next < 3 or m < KD - 1:
                                add_square(m, n_next)

            def take_out(w):
                what, pair, g = mix_kind(w)
                if w - 2 >= MIX:
                    dve.wait_ge(op_lo_done, w - 2 - MIX + 1)
                dve.wait_ge(unit_done, w + 1)
                if what == "q":
                    dve.scalar_tensor_tensor(raw[:, w % 2, :], acc[w % RING][:], HD ** -0.5, rstd[:], ALU.mult,
                                             ALU.mult).then_inc(raw_done, 1)
                elif what == "rv":
                    dve.tensor_tensor(raw[:, w % 2, :].rearrange("c (r p) -> c p r", r=DIL),
                                      acc[w % RING][:].rearrange("c (p r) -> c p r", r=DIL),
                                      rstd[:].rearrange("c (p r) -> c p r", r=DIL), ALU.mult).then_inc(raw_done, 1)
                else:
                    dve.tensor_tensor(raw[:, w % 2, :], acc[w % RING][:], rstd[:], ALU.mult).then_inc(raw_done, 1)

            dve.memset(ones[:], 1.0).then_inc(consts_made, 1)
            dve.wait_ge(gains_loaded, 16)
            for kind, w in START_STEPS:
                if kind == "x":
                    dve.wait_ge(x_loaded[w], 16)
                    prep(w, 0)
                elif kind == "sq":
                    add_square(w, 0)
                else:
                    (u, half) = w
                    dve.wait_ge(whi_done if half else half_hi_done, u + 1)
                    dve.tensor_tensor(w_lo[:, u, half_cols(half)], w_raw[:, u, half_cols(half)],
                                      w_hi[:, u, half_cols(half)].bitcast(F32),
                                      ALU.subtract).then_inc(wlo_done if half else half_lo_done, 1)
            dve.wait_ge(const_loaded, 16 * N_CONST)
            dve.tensor_scalar(hbias[:], bias[:], 0.5, None, ALU.mult).then_inc(hbias_made, 1)
            dve.memset(negones[:].bitcast(F32), -1.0).then_inc(consts_made, 1)
            dve.tensor_copy(tri[:], trif).then_inc(consts_made, 1)
            dve.wait_ge(consts_made, 3)
            ffn(FFN_A, 0, 0, 1)

            for kind, w in MIX_STEPS:
                if kind == "Ua":
                    if not POOL_LO[0] <= w + 2 < POOL_LO[1]:
                        split_lo(w + 2, 0, unit_width(w + 2))
                elif kind == "norm":
                    norm(w)
                    take_out(MIX)
                elif kind == "gate":
                    dve.wait_ge(unit_done, w + 1)
                    dve.wait_ge(pv_done, 2 * SB_PAIRS + 2)
                    dve.tensor_tensor(gsb[:, w - GATE, :], acc[w % RING][:], rstd[:],
                                      ALU.mult).then_inc(acc_read[w % RING], 1)
                elif kind == "Ub":
                    if MIX < w < GATE:
                        take_out(w)
                elif kind == "fin":
                    what, pair, g = mix_kind(w)
                    n = w - MIX
                    fin = n + 1
                    src = raw[:, w % 2, :]
                    if what in "qk":
                        hi, lo = (sq_hi, sq_lo) if what == "q" else (sk_hi, sk_lo)
                        dve.wait_ge(op_hi_done, fin)
                        dve.tensor_tensor(lo[:, pair % 2, :], src, hi[:, pair % 2, :].bitcast(F32),
                                          ALU.subtract).then_inc(op_lo_done, 1)
                    elif what in ("rq", "rk"):
                        t = ROPES.index(w)
                        if t:
                            dve.wait_ge(op_lo_done, n)
                        dve.wait_ge(raw_done, fin)
                        dve.tensor_tensor(rope1[:], src, cos[:], ALU.mult).then_inc(rope_step, 1)
                        dve.wait_ge(rope_step, 2 * t + 1)
                        dve.wait_ge(rotated, 4 * (t + 1))
                        dve.tensor_tensor(roped[:].rearrange("c (r p) -> c p r", r=DIL),
                                          rope1[:].rearrange("c (p r) -> c p r", r=DIL),
                                          rope2[:].rearrange("c (p r) -> c p r", r=DIL),
                                          ALU.add).then_inc(rope_step, 1)
                        hi = dq_hi[pair][:, g, :] if what == "rq" else dk_hi[pair][:]
                        lo = dq_lo[pair][:, g, :] if what == "rq" else dk_lo[pair][:]
                        dve.wait_ge(rope_step, 2 * t + 2)
                        dve.wait_ge(op_hi_done, fin)
                        dve.tensor_tensor(lo, roped[:], hi.bitcast(F32), ALU.subtract).then_inc(op_lo_done, 1)
                    else:
                        hi, lo = v_parts(sv[:, pair % 2, :, :] if what == "v" else dv[pair][:])
                        dve.wait_ge(op_hi_done, fin)
                        dve.tensor_tensor(lo,
                                          acc[w % RING][:].rearrange("p (b a c) -> p b a c", b=BLK, a=2),
                                          hi.bitcast(F32), ALU.subtract).then_inc(op_lo_done, 1)
                elif kind == "scores":
                    for b in range(3):
                        t = 3 * w + b
                        cols = slice(SB_AT[b], SB_AT[b] + SB_WIDTH[b])
                        dve.wait_ge(soft_step, 3 * t + 3)
                        dve.scalar_tensor_tensor(ebuf[:, cols], bank[b][:, 0:SB_WIDTH[b]], 0.0, ebuf[:, cols],
                                                 ALU.max, ALU.add).then_inc(sp_step, 1)
                        dve.wait_ge(sp_step, 2 * t + 1)
                        if w:
                            dve.wait_ge(pv_done, w)
                        dve.tensor_copy(spA_hi[:, cols], ebuf[:, cols]).then_inc(sp_step, 1)
                        dve.wait_ge(sp_step, 2 * t + 2)
                        dve.tensor_tensor(spA_lo[:, cols], ebuf[:, cols], spA_hi[:, cols].bitcast(F32),
                                          ALU.subtract).then_inc(sp_split, 1)
                elif kind == "suffix":
                    for b in range(3):
                        t = 3 * w + b
                        cols = slice(SB_AT[b], SB_AT[b] + SB_WIDTH[b])
                        dve.wait_ge(a_done, t + 1)
                        dve.wait_ge(suffix_done, 3 * w + 3)
                        dve.tensor_copy(spA_hi[:, cols], ebuf[:, cols]).then_inc(a_hi_done, 1)
                        dve.wait_ge(a_hi_done, t + 1)
                        dve.tensor_tensor(spA_lo[:, cols], ebuf[:, cols], spA_hi[:, cols].bitcast(F32),
                                          ALU.subtract).then_inc(a_split, 1)
                elif kind in ("y", "dy"):
                    rows = head_rows(w)
                    n = w + (2 * SB_PAIRS if kind == "dy" else 0)
                    dve.wait_ge(y_cross_done, n + 1)
                    dve.tensor_tensor(ysum[rows, :], ysum[rows, :], bank[3][rows, :], ALU.add).then_inc(y_whole, 1)
                elif kind == "ysplit":
                    rows = head_rows(w)
                    dve.wait_ge(y_whole, w + 1)
                    dve.wait_ge(ys_hi_done, w + 1)
                    dve.tensor_tensor(ys_lo[rows, w // 2, :], ysum[rows, :], ys_hi[rows, w // 2, :].bitcast(F32),
                                      ALU.subtract).then_inc(ys_done, 1)
                elif kind == "dysplit":
                    rows = head_rows(w)
                    natural = lambda t: t[rows, w // 2, :].rearrange("c (p r) -> c r p", r=DIL)
                    dve.wait_ge(y_whole, 2 * SB_PAIRS + w + 1)
                    dve.wait_ge(ys_hi_done, 2 * SB_PAIRS + w + 1)
                    dve.tensor_tensor(natural(yd_lo), ysum[rows, :].rearrange("c (r p) -> c r p", r=DIL),
                                      natural(yd_hi).bitcast(F32), ALU.subtract).then_inc(ys_done, 1)
                elif kind == "dscores":
                    j, r = w
                    n = DIL * j + r
                    t = stats[:, n % 2, :]
                    dve.wait_ge(ds_done, n + 1)
                    dve.tensor_reduce(t[:, 0:1], pair_bank[:, 0:6 * P], AX.X, ALU.max).then_inc(max_step, 1)
                    dve.wait_ge(max_step, 2 * n + 1)
                    dve.tensor_scalar(t[:, 1:2], t[:, 0:1], -HD ** -0.5, None, ALU.mult).then_inc(max_step, 1)
                elif kind == "dadd":
                    j, r = w
                    n = DIL * j + r
                    t = stats[:, n % 2, :]
                    p = prob[:, n % 2, :]
                    own = p[:, r * P:(r + 1) * P]
                    dve.wait_ge(p_done, n + 1)
                    dve.reciprocal(t[:, 3:4], t[:, 2:3]).then_inc(p_step, 1)
                    dve.wait_ge(p_step, 4 * n + 1)
                    dve.tensor_scalar(p[:, 0:SEQ], p[:, 0:SEQ], t[:, 3:4], None, ALU.mult).then_inc(p_step, 1)
                    for g in (1, 2):
                        dve.wait_ge(p_step, 4 * n + 1 + g)
                        dve.scalar_tensor_tensor(own, p[:, SEQ + (g - 1) * P:SEQ + g * P], t[:, 3:4], own,
                                                 ALU.mult, ALU.add).then_inc(p_step, 1)
                elif kind == "dlo":
                    j, r = w
                    n = DIL * j + r
                    if r == 0 and j:
                        dve.wait_ge(pv_done, 2 * SB_PAIRS + j)
                    dve.wait_ge(pt_hi_done, n + 1)
                    dve.tensor_tensor(pT_lo[:, :, r * P:(r + 1) * P], bank[2].rearrange("p (b c) -> p b c", b=DIL),
                                      pT_hi[:, :, r * P:(r + 1) * P].bitcast(F32), ALU.subtract).then_inc(pt_split, 1)

            for i in range(KD // 4):
                for j in range(12):
                    u, v = END + j, END + 12 * i + j + 2
                    s = u % RING
                    m = 4 * i + j // 3
                    split_lo(v, 0, unit_width(v))
                    dve.wait_ge(unit_done, 12 * i + (u + 1))
                    if j % 3 == 0:
                        dve.tensor_tensor(gdl[:, j // 3 % 2, :], acc[s][:], rstd[:], ALU.mult).then_inc(acc_read[s], 1)
                    elif j % 3 == 1:
                        if m:
                            dve.wait_ge(mg_lo_done, m)
                        dve.scalar_tensor_tensor(part[:, 0, :], gsb[:, m, :], 1.0, acc[s][:], ALU.add,
                                                 ALU.mult).then_inc(acc_read[s], 1)
                    else:
                        dve.wait_ge(gate_done, m + (KD + 1))
                        dve.scalar_tensor_tensor(part[:, 1, :], gdl[:, j // 3 % 2, :], 1.0, acc[s][:], ALU.add,
                                                 ALU.mult).then_inc(acc_read[s], 1)
                        dve.wait_ge(acc_read[s], reads(u, 3 * i) + 1)
                        dve.wait_ge(acc_read[(u - 1) % RING], reads(u - 1, 3 * i) + 1)
                        dve.tensor_tensor(part[:, 0, :], part[:, 0, :], part[:, 1, :], ALU.add).then_inc(merge_step, 1)
                        dve.wait_ge(merge_step, m + 1)
                        dve.wait_ge(mg_hi_done, m + 1)
                        dve.scalar_tensor_tensor(mg_lo[:, m, :], part[:, 0, :], 0.5, mg_hi[:, m, :].bitcast(F32),
                                                 ALU.mult, ALU.subtract).then_inc(mg_lo_done, 1)
            for m in range(KD):
                split_lo(WO + m + 2, 0, KD * P)
                s, before = update_x(WO + m, m, 1.0)
                dve.wait_ge(acc_read[s], before + 1)
                prep(m, 2)
                add_square(m, 2)
            ffn(FFN_B, NF, 2, 3)
            dve.wait_ge(sumsq_done, 4)
            dve.tensor_scalar(col[:], bank[2][:, 0:BLK], 1.0 / D, EPS, ALU.mult, ALU.add).then_inc(mean_done, 1)
            dve.wait_ge(rms_done, 4)
            dve.reciprocal(col[:], col[:]).then_inc(rstd_done, 1)
            dve.wait_ge(rstd_done, 4)
            for b in range(BLK):
                dve.tensor_scalar(diag[:, b * P:(b + 1) * P], identf[:], col[:, b:b + 1], None,
                                  ALU.mult).then_inc(diag_done, 1)
            dve.wait_ge(spread_done, 1)
            for m in range(KD):
                dve.scalar_tensor_tensor(x[:, m, :], x[:, m, :], gains[:, 3, m:m + 1], bank[0], ALU.mult,
                                         ALU.mult).then_inc(y_ready, 1)

        @block.gpsimd
        def _(pool):
            pool.wait_ge(const_loaded, 16 * N_CONST)
            half = HD // 2
            for kind, w in MIX_STEPS:
                v = w + 2 if kind == "Ua" else 0
                if POOL_LO[0] <= v < POOL_LO[1]:
                    s, width = v % RING, unit_width(v)
                    pool.wait_ge(whi_done, v + 1)
                    pool.wait_ge(unit_done, v - RING + 1)
                    if ropes_before(v - 2):
                        pool.wait_ge(rotated, 4 * ropes_before(v - 2))
                    pool.tensor_tensor(w_lo[:, s, 0:width], w_raw[:, s, 0:width], w_hi[:, s, 0:width].bitcast(F32),
                                       ALU.subtract).then_inc(pool_lo_done, 1)
                if kind == "Ub" and w in ROPES:
                    t = ROPES.index(w)
                    pool.wait_ge(raw_done, w - MIX + 1)
                    if w + 2 >= POOL_LO[0]:
                        pool.wait_ge(pool_lo_done, w + 3 - POOL_LO[0])
                    if t:
                        pool.wait_ge(rope_step, 2 * t)
                    for c in range(0, P, half):
                        to = c + half if c % HD == 0 else c - half
                        pool.tensor_tensor(rope2[to:to + half, :], raw[c:c + half, w % 2, :], sin[c:c + half, :],
                                           ALU.mult).then_inc(rotated, 1)

        @block.tensor
        def _(pe):
            def product(o, w_h, w_l, r_h, r_l, first, last, check=False):
                pe.matmul(o, w_h, r_h, start=first, stop=False, skip_group_check=check)
                pe.matmul(o, w_h, r_l, start=False, stop=False, skip_group_check=check)
                return pe.matmul(o, w_l, r_h, start=False, stop=last, skip_group_check=check)

            def pv_product(h, v, a_h, a_l, col, first, last):
                a = h % 2
                pe.matmul(bank[3][:, col:SEQ], v[:, P * a:P * (a + 1)], a_h, start=first, stop=False,
                          skip_group_check=True)
                return pe.matmul(bank[3][0:HD, col:SEQ], v[:, P * a:P * a + HD], a_l, start=False, stop=last,
                                 skip_group_check=True)

            def bank_free(u0, i):
                last = u0 - RING
                if last < 0 and isinstance(i, int):
                    return
                if not MIX <= last < GATE:
                    pe.wait_ge(acc_read[u0 % RING], reads(u0, i))
                    return
                kind = mix_kind(last)[0]
                if kind in ("q", "k", "rq", "rk"):
                    pe.wait_ge(raw_done, last - MIX + 1)
                else:
                    pe.wait_ge(op_lo_done, last - MIX + 1)

            def unit(u0, i, rhs, ks, before=None, half=None):
                s = u0 % RING
                n = len(ks)
                lo, hi = {None: (0, n), 0: (0, n // 2), 1: (n // 2, n)}[half]
                if half != 1 or u0 < RING:
                    wait_lo(pe, u0, i)
                    bank_free(u0, i)
                for k in range(lo, hi):
                    if before:
                        before(k)
                    r_h, r_l = rhs(ks[k])
                    mm = product(acc[s][:], w_hi[:, s, k * P:(k + 1) * P], w_lo[:, s, k * P:(k + 1) * P], r_h, r_l,
                                 k == 0, k == n - 1)
                if half != 0:
                    mm.then_inc(unit_done, 1)

            xg = lambda k: (xg_hi[:, k, :], xg_lo[:, k, :])
            hid = lambda k: (hid_hi[:, k, :], hid_lo[:, k, :])
            K8 = list(range(KD))

            def norm(n):
                pe.wait_ge(sum_done, (KD - 1) * (n + 1))
                pe.matmul(bank[0], ones[:], ssum[:], start=True, stop=True).then_inc(sumsq_done, 1)

            def ffn(base, fb, n_norm):
                for c, (f0, n) in enumerate(CHUNKS):
                    u = chunk_base(base, c)
                    lo = 0
                    if c == 0:
                        lo = 1
                        if n_norm:
                            unit(u, 0, xg, K8, lambda k: pe.wait_ge(xg_lo_done, KD * n_norm + k + 1))
                            norm(n_norm)
                            for j in (1, 2, 3):
                                unit(u + j, 0, xg, K8)
                        else:
                            for k in range(KD // 2):
                                pe.wait_ge(xg_lo_done, k + 1)
                                for j in range(RING):
                                    if k == 0:
                                        pe.wait_ge(half_lo_done, j + 1)
                                    cols = slice(k * P, (k + 1) * P)
                                    product(acc[j][:], w_hi[:, j, cols], w_lo[:, j, cols], *xg(k), k == 0, False)
                            for j in range(RING):
                                unit(u + j, 0, xg, K8, lambda k: pe.wait_ge(xg_lo_done, k + 1), half=1)
                                if j == 0:
                                    norm(n_norm)
                    with pe.Fori(lo, n // 2) as i:
                        for j in range(4):
                            unit(u + j, i, xg, K8)
                    u += 2 * n
                    ks = list(range(n))
                    for m in range(4):
                        unit(u + m, 0, hid, ks, (lambda k: pe.wait_ge(hid_lo_done, fb + f0 + k + 1)) if m == 0 else None)
                    for m in range(4, 8):
                        unit(u + m, 0, hid, ks)

            pe.wait_ge(consts_made, 1)
            ffn(FFN_A, 0, 0)

            for kind, w in MIX_STEPS:
                if kind == "Ua":
                    unit(w, 0, xg, K8, (lambda k: pe.wait_ge(xg_lo_done, KD + k + 1)) if w == MIX else None, half=0)
                elif kind == "Ub":
                    unit(w, 0, xg, K8, (lambda k: pe.wait_ge(xg_lo_done, KD + k + 1)) if w == MIX else None, half=1)
                elif kind == "norm":
                    norm(w)
                elif kind == "fin":
                    what, pair, g = mix_kind(w)
                    if what not in ("v", "rv"):
                        continue
                    pe.wait_ge(raw_done, w - MIX + 1)
                    for b in range(BLK):
                        mm = pe.transpose(acc[w % RING][:, b * P:(b + 1) * P], raw[:, w % 2, b * P:(b + 1) * P],
                                          identf[:])
                    mm.then_inc(turned, 1)
                elif kind == "scores":
                    hp, a = w // 2, w % 2
                    rows = slice(HD * a, HD * a + HD)
                    pe.wait_ge(op_lo_done, through(("q", hp, 0), ("k", hp, 0)))
                    if w == 0:
                        pe.wait_ge(mean_done, 2)
                        pe.wait_ge(consts_made, 3)
                        pe.wait_ge(const_loaded, 16 * N_CONST)
                    for b, parts in enumerate(SB_BANKS):
                        if w:
                            pe.wait_ge(a_done, 3 * (w - 1) + b + 1)
                        for n, (i, col) in enumerate(parts):
                            o = bank[b][:, col:col + SEQ - P * i]
                            ks = slice(P * i, P * i + P)
                            product(o, sk_hi[rows, hp % 2, ks], sk_lo[rows, hp % 2, ks],
                                    sq_hi[rows, hp % 2, P * i:SEQ], sq_lo[rows, hp % 2, P * i:SEQ],
                                    n == 0, False, True)
                        for i, col in parts:
                            mm = pe.matmul(bank[b][:, col:col + P], identb[:], mask_sb[:], start=False, stop=False,
                                           skip_group_check=True)
                        mm.then_inc(z_done, 1)
                elif kind == "suffix":
                    for b, parts in enumerate(SB_BANKS):
                        need = (2, 2, 3)[b]
                        pe.wait_ge(sp_split, 3 * w + need)
                        for i, col in parts:
                            for j in range(i, BLK):
                                bj, cj = sb_block(j)
                                at = slice(SB_AT[bj] + cj, SB_AT[bj] + cj + SEQ - P * j)
                                o = bank[b][:, col + P * (j - i):col + SEQ - P * i]
                                m = tri if i == j else negones
                                pe.matmul(o, m[:], spA_hi[:, at], start=False, stop=False, skip_group_check=True)
                                mm = pe.matmul(o, m[:], spA_lo[:, at], start=False, stop=True, skip_group_check=True)
                        mm.then_inc(suffix_done, 1)
                elif kind == "pv":
                    hp = w // 2
                    pe.wait_ge(op_lo_done, through(("v", hp, 0)))
                    pe.wait_ge(a_split, 3 * w + 3)
                    if w:
                        pe.wait_ge(y_whole, w)
                    for i in range(BLK):
                        b, col = sb_block(i)
                        at = slice(SB_AT[b] + col, SB_AT[b] + col + SEQ - P * i)
                        mm = pv_product(w, sv[:, hp % 2, i, :], spA_hi[:, at], spA_lo[:, at], P * i, i == 0,
                                        i == BLK - 1)
                    mm.then_inc(pv_done, 1)
                elif kind == "dscores":
                    j, r = w
                    jp, n = j // 2, DIL * j + r
                    rows = slice(HD * (j % 2), HD * (j % 2) + HD)
                    own = slice(r * P, (r + 1) * P)
                    pe.wait_ge(op_lo_done, through(("rq", jp, NG - 1), ("rk", jp, 0)))
                    if n:
                        pe.wait_ge(p_done, n)
                    else:
                        pe.wait_ge(a_done, 6 * SB_PAIRS)
                    product(bank[0], dq_hi[jp][rows, 0, own], dq_lo[jp][rows, 0, own], dk_hi[jp][rows, :],
                            dk_lo[jp][rows, :], True, False, True)
                    for g in (1, 2):
                        product(bank[1][:, (g - 1) * P:g * P], dq_hi[jp][rows, g, own], dq_lo[jp][rows, g, own],
                                dk_hi[jp][rows, own], dk_lo[jp][rows, own], g == 1, False, True)
                    pe.matmul(bank[0], identb[:], mask_g0[:, r, :], start=False, stop=True, skip_group_check=True)
                    pe.matmul(bank[1][:, 0:2 * P], identb[:], mask_g12[:], start=False, stop=True,
                              skip_group_check=True).then_inc(ds_done, 1)
                elif kind == "dturn":
                    j, r = w
                    n = DIL * j + r
                    pe.wait_ge(p_step, 4 * n + 4)
                    if n:
                        pe.wait_ge(pt_split, n)
                    for b in range(DIL):
                        mm = pe.transpose(bank[2][:, b * P:(b + 1) * P], prob[:, n % 2, b * P:(b + 1) * P], identf[:])
                    mm.then_inc(pt_turned, 1)
                elif kind == "dpv":
                    jp = w // 2
                    pe.wait_ge(op_lo_done, through(("rv", jp, 0)))
                    pe.wait_ge(pt_split, DIL * (w + 1))
                    pe.wait_ge(y_whole, 2 * SB_PAIRS + w)
                    for b in range(DIL):
                        mm = pv_product(w, dv[jp][:, b, :], pT_hi[:, b, :], pT_lo[:, b, :], 0, b == 0, b == DIL - 1)
                    mm.then_inc(pv_done, 1)

            ys = lambda k: (ys_hi[:, k, :], ys_lo[:, k, :])
            yd = lambda k: (yd_hi[:, k, :], yd_lo[:, k, :])
            with pe.Fori(0, KD // 4) as i:
                for j in range(0, 12, 3):
                    unit(END + j, 3 * i, xg, K8)
                    if j == 0:
                        pe.wait_ge(ys_done, 2 * (SB_PAIRS + DL_PAIRS))
                    unit(END + j + 1, 3 * i, ys, K8[0:SB_PAIRS])
                    unit(END + j + 2, 3 * i, yd, K8[0:DL_PAIRS])
            for m in range(KD):
                unit(WO + m, 0, lambda k: (mg_hi[:, k, :], mg_lo[:, k, :]), K8,
                     (lambda k: pe.wait_ge(mg_lo_done, k + 1)) if m == 0 else None)
            ffn(FFN_B, NF, 2)
            for part_sum, sm, count in ((ssum[:], sum_done, 3 * (KD - 1) + KD - 2), (sq[:, (KD - 1) % 2, :], sq_done, 4 * KD)):
                pe.wait_ge(sm, count)
                for b in range(BLK):
                    last = sm is sq_done and b == BLK - 1
                    mm = pe.matmul(bank[2][:, b:b + 1], part_sum[:, b * P:(b + 1) * P], ones[:, 0:1],
                                   start=sm is sum_done and b == 0, stop=last, skip_group_check=True)
            mm.then_inc(sumsq_done, 1)
            for b in range(BLK):
                pe.wait_ge(diag_done, b + 1)
                mm = pe.matmul(bank[0][:, b * P:(b + 1) * P], ones[:], diag[:, b * P:(b + 1) * P], start=b == 0,
                               stop=b == BLK - 1, skip_group_check=True)
            mm.then_inc(spread_done, 1)


def constants():
    half = HD // 2
    inv = (np.float32(10000.0) ** (-np.arange(half, dtype=np.float32) / np.float32(half))).astype(np.float32)
    ang = (np.arange(SEQ, dtype=np.float32)[:, None] * inv[None, :]).astype(np.float32).T
    row = np.arange(P) % half
    sign = np.where(np.arange(P) % HD < half, 1.0, -1.0)[:, None]
    i = np.arange(P)
    t = DIL * i[:, None, None, None] + np.arange(DIL)[None, :, None, None]
    s = DIL * i[None, None, None, :] + np.arange(DIL)[None, None, :, None]
    ok0 = (t - s >= 0) & (t - s <= P)
    back = i[:, None] - i[None, :]
    ok12 = np.concatenate([back >= 0, (back >= 0) & (back % 4 == 0)], 1)

    def bf16_bits(v):
        return (np.asarray(v, np.float32).view(np.uint32) >> 16).astype(np.uint16)

    return {
        "cos": np.cos(ang.astype(np.float64)).astype(np.float32)[row],
        "sin": np.sin(ang.astype(np.float64)).astype(np.float32)[row] * sign.astype(np.float32),
        "identf": np.eye(P, dtype=np.float32),
        "trif": -(i[:, None] >= i[None, :]).astype(np.float32),
        "identb": bf16_bits(np.eye(P)),
        "mask_sb": bf16_bits(np.where(i[:, None] < i[None, :], 0.0, NEG)),
        "mask_g0": bf16_bits(np.where(ok0, 0.0, NEG)).reshape(P, DIL, SEQ),
        "mask_g12": bf16_bits(np.where(ok12, 0.0, NEG)),
    }


def kernel(**inputs):
    import concourse.bacc as bacc
    from concourse.bass_utils import run_bass_kernel_spmd

    a = {k: np.asarray(v) for k, v in inputs.items()}

    def units(w):
        k, m = w.shape
        return w.reshape(k // P, P, m // P, P).transpose(2, 1, 0, 3).reshape(m // P, P, k)

    def pairs(w1, w3):
        return np.stack([units(w1), units(w3)], 1).reshape(2 * NF, P, D)

    win = units(a["w_in"][0])
    SBT, DQT = SB_PAIRS, NG * DL_PAIRS
    first = {"q": 0, "k": SBT, "v": 2 * SBT, "rq": 3 * SBT, "rk": 3 * SBT + DQT, "rv": 3 * SBT + DQT + DL_PAIRS}
    order = [first[what] + DL_PAIRS * g + pair for what, pair, g in MIX_ORDER]
    gate0 = first["rv"] + DL_PAIRS
    wend = np.concatenate([win[gate0 + KD:gate0 + 2 * KD], units(a["w_sb_out"][0]),
                           units(a["w_dil_out"][0])], 2)
    cols = lambda v: v.reshape(-1, P).T
    arrays = {
        "xT": a["x"][0].T.reshape(KD, P, SEQ).transpose(1, 0, 2),
        "gains": np.stack([cols(a[n].reshape(-1)) for n in ("g_ffn1", "g_mix", "g_ffn2", "g_final")], 1),
        "bias": cols(a["b_gate"][0]).reshape(P, 2, KD),
        "w13a": pairs(a["w1_a"][0], a["w3_a"][0]), "w2a": units(a["w2_a"][0]),
        "w13b": pairs(a["w1_b"][0], a["w3_b"][0]), "w2b": units(a["w2_b"][0]),
        "wmix": win[order], "wgate": win[gate0:gate0 + KD], "wend": wend, "wo": units(a["w_o"][0]),
    }
    arrays.update(constants())
    arrays = {k: np.ascontiguousarray(v) for k, v in arrays.items()}

    nc = bacc.Bacc("TRN2", target_bir_lowering=False, num_devices=1)
    A = {n: nc.dram_tensor("in_" + n, v.shape, mybir.dt.from_np(v.dtype), kind="ExternalInput").ap()
         for n, v in arrays.items()}
    out = nc.dram_tensor("out", (P, KD, SEQ), mybir.dt.float32, kind="ExternalOutput").ap()
    build(nc, A, out)
    r = run_bass_kernel_spmd(nc, [{"in_" + n: v for n, v in arrays.items()}], core_ids=[0])
    y = r.results[0]["out"]
    return np.ascontiguousarray(y.transpose(1, 0, 2).reshape(1, D, SEQ).transpose(0, 2, 1))
```
